# Optimizing a Trainium2 kernel written in Bass

```python
import jax
import jax.numpy as jnp
from jax import lax
import numpy as np

D_MODEL = 1024
BATCH = 1
SEQ = 512
DEPTH = 2
DEC_BATCH = 8
DEC_SEQ = 4
PAST_LEN = 2048
PAGE_SIZE = 128

N_AB_LAYERS = (DEPTH + 1) // 2
N_C_LAYERS = DEPTH // 2

A_HEADS = 8
A_HEAD_DIM = 64
A_WIDTH = A_HEADS * A_HEAD_DIM
Q_BLOCK = 128
B_WIDTH = D_MODEL // 2
B_CONV = 3
AB_IN_WIDTH = 3 * A_WIDTH + A_HEADS + 3 * B_WIDTH
AB_OUT_WIDTH = A_WIDTH + B_WIDTH
C_HEADS = 8
C_KEY_DIM = 128
C_VAL_DIM = 128
C_QK_WIDTH = C_HEADS * C_KEY_DIM
C_V_WIDTH = C_HEADS * C_VAL_DIM
C_CONV = 4
C_CONV_WIDTH = 2 * C_QK_WIDTH + C_V_WIDTH
C_IN_WIDTH = C_CONV_WIDTH + C_V_WIDTH + 2 * C_HEADS
C_CHUNK = 64
D_FF = 2816
NORM_EPS = 1e-6
DT_MIN = 1e-3
DT_MAX = 1e-1

kernel_name = 'fox_shortconv_gdn_macaron_decode_step'

def rmsnorm(x, g):
    xf = x.astype(jnp.float32)
    y = xf * lax.rsqrt(jnp.mean(xf * xf, axis=-1, keepdims=True) + NORM_EPS)
    return (y * g.astype(jnp.float32)).astype(x.dtype)

def l2norm(x):
    xf = x.astype(jnp.float32)
    return xf * lax.rsqrt(jnp.sum(xf * xf, axis=-1, keepdims=True) + NORM_EPS)

def swiglu(x, w_gate, w_up, w_down):
    return (jax.nn.silu(x @ w_gate) * (x @ w_up)) @ w_down

def causal_depthwise_conv(u, buf, w):
    width = w.shape[0]
    length = u.shape[1]
    ext = jnp.concatenate([buf.astype(u.dtype), u], axis=1)
    out = ext[:, 0:length] * w[0]
    for j in range(1, width):
        out = out + ext[:, j:j + length] * w[j]
    return out, ext[:, length:]

def gather_pages(pool, layer, page_table):
    g = pool[layer, page_table]
    return g.reshape((g.shape[0], g.shape[1] * g.shape[2]) + g.shape[3:])

def fox_attention(q, k, v, logf, q_offset):
    bsz, lq, h, d = q.shape
    lk = k.shape[1]
    c_k = jnp.cumsum(logf.astype(jnp.float32), axis=1).transpose(0, 2, 1)
    qb = min(Q_BLOCK, lq)
    nb = lq // qb
    scale = d ** -0.5
    q_blocks = q.reshape(bsz, nb, qb, h, d).transpose(1, 0, 2, 3, 4)
    pos_blocks = (q_offset + jnp.arange(lq)).reshape(nb, qb)
    key_pos = jnp.arange(lk)

    def block(args):
        q_blk, q_pos = args
        s = jnp.einsum('bqhd,bkhd->bhqk', q_blk, k).astype(jnp.float32) * scale
        c_q = jnp.take(c_k, q_pos, axis=2)
        s = s + c_q[..., :, None] - c_k[..., None, :]
        s = jnp.where(key_pos[None, :] <= q_pos[:, None], s, -jnp.inf)
        p = jax.nn.softmax(s, axis=-1).astype(v.dtype)
        return jnp.einsum('bhqk,bkhd->bqhd', p, v)

    o = lax.map(block, (q_blocks, pos_blocks))
    return o.transpose(1, 0, 2, 3, 4).reshape(bsz, lq, h, d)

def gated_delta_rule(q, k, v, g, beta, s0):
    bsz, length, h, dk = q.shape
    dv = v.shape[-1]
    cs = min(C_CHUNK, length)
    pad = (-length) % cs
    if pad:
        pw = ((0, 0), (0, pad), (0, 0), (0, 0))
        q = jnp.pad(q, pw)
        k = jnp.pad(k, pw)
        v = jnp.pad(v, pw)
        g = jnp.pad(g, pw[:3])
        beta = jnp.pad(beta, pw[:3])
    n = (length + pad) // cs

    def chunks(t):
        t = t.reshape((bsz, n, cs) + t.shape[2:])
        return jnp.moveaxis(t, 3, 2).swapaxes(0, 1)

    qc, kc, vc, gc, bc = chunks(q), chunks(k), chunks(v), chunks(g), chunks(beta)
    G = jnp.cumsum(gc, axis=-1)
    incl = jnp.tril(jnp.ones((cs, cs), dtype=bool))
    strict = jnp.tril(jnp.ones((cs, cs), dtype=bool), -1)
    diff = G[..., :, None] - G[..., None, :]
    decay = jnp.where(incl, jnp.exp(jnp.where(incl, diff, 0.0)), 0.0)
    kk = jnp.einsum('nbhtd,nbhsd->nbhts', kc, kc)
    a_mat = jnp.where(strict, bc[..., :, None] * kk * decay, 0.0) + jnp.eye(cs, dtype=jnp.float32)
    w_v = lax.linalg.triangular_solve(a_mat, bc[..., None] * vc, left_side=True, lower=True, unit_diagonal=True)
    w_k = lax.linalg.triangular_solve(a_mat, (bc * jnp.exp(G))[..., None] * kc, left_side=True, lower=True, unit_diagonal=True)
    p = jnp.einsum('nbhtd,nbhsd->nbhts', qc, kc) * decay
    q_dec = jnp.exp(G)[..., None] * qc
    k_dec = jnp.exp(G[..., -1:] - G)[..., None] * kc
    g_last = jnp.exp(G[..., -1])

    def step(s, xs):
        w_v_c, w_k_c, p_c, q_dec_c, k_dec_c, gl = xs
        u = w_v_c - jnp.einsum('bhtk,bhvk->bhtv', w_k_c, s)
        o = jnp.einsum('bhtk,bhvk->bhtv', q_dec_c, s) + jnp.einsum('bhts,bhsv->bhtv', p_c, u)
        s = gl[..., None, None] * s + jnp.einsum('bhtv,bhtk->bhvk', u, k_dec_c)
        return s, o

    s_final, o = lax.scan(step, s0, (w_v, w_k, p, q_dec, k_dec, g_last))
    o = jnp.moveaxis(o.swapaxes(0, 1), 2, 3).reshape(bsz, n * cs, h, dv)[:, :length]
    return o, s_final

def mixer_ab(h, w_in, b_f, conv_w, w_out, past_kvf, conv_buf):
    bsz, length, _ = h.shape
    proj = h @ w_in
    splits = [A_WIDTH, 2 * A_WIDTH, 3 * A_WIDTH, 3 * A_WIDTH + A_HEADS,
              3 * A_WIDTH + A_HEADS + B_WIDTH, 3 * A_WIDTH + A_HEADS + 2 * B_WIDTH]
    q, k, v, f_pre, gate_b, gate_c, u = jnp.split(proj, splits, axis=-1)
    q = q.reshape(bsz, length, A_HEADS, A_HEAD_DIM)
    k = k.reshape(bsz, length, A_HEADS, A_HEAD_DIM)
    v = v.reshape(bsz, length, A_HEADS, A_HEAD_DIM)
    logf = jax.nn.log_sigmoid(f_pre.astype(jnp.float32) + b_f.astype(jnp.float32))
    if past_kvf is None:
        k_all, v_all, logf_all, q_offset = k, v, logf, 0
    else:
        k_past, v_past, logf_past = past_kvf
        k_all = jnp.concatenate([k_past, k], axis=1)
        v_all = jnp.concatenate([v_past, v], axis=1)
        logf_all = jnp.concatenate([logf_past.astype(jnp.float32), logf], axis=1)
        q_offset = k_past.shape[1]
    o_a = fox_attention(q, k_all, v_all, logf_all, q_offset).reshape(bsz, length, A_WIDTH)
    y_conv, new_buf = causal_depthwise_conv(gate_c * u, conv_buf, conv_w)
    o_b = gate_b * y_conv
    out = jnp.concatenate([o_a, o_b.astype(o_a.dtype)], axis=-1) @ w_out
    return out, (k, v, logf, new_buf)

def mixer_c(h, w_in, conv_w, a_log, dt_bias, norm_w, w_out, conv_buf, s0):
    bsz, length, _ = h.shape
    proj = h @ w_in
    qkv, z, b_pre, a_pre = jnp.split(proj, [C_CONV_WIDTH, C_CONV_WIDTH + C_V_WIDTH, C_CONV_WIDTH + C_V_WIDTH + C_HEADS], axis=-1)
    qkv_c, new_buf = causal_depthwise_conv(qkv, conv_buf, conv_w)
    qkv_c = jax.nn.silu(qkv_c)
    q, k, v = jnp.split(qkv_c, [C_QK_WIDTH, 2 * C_QK_WIDTH], axis=-1)
    q = l2norm(q.reshape(bsz, length, C_HEADS, C_KEY_DIM)) * (C_KEY_DIM ** -0.5)
    k = l2norm(k.reshape(bsz, length, C_HEADS, C_KEY_DIM))
    v = v.reshape(bsz, length, C_HEADS, C_VAL_DIM).astype(jnp.float32)
    beta = jax.nn.sigmoid(b_pre.astype(jnp.float32))
    g = -jnp.exp(a_log.astype(jnp.float32)) * jax.nn.softplus(a_pre.astype(jnp.float32) + dt_bias.astype(jnp.float32))
    o, s_new = gated_delta_rule(q, k, v, g, beta, s0.astype(jnp.float32))
    o = rmsnorm(o, norm_w) * jax.nn.silu(z.reshape(bsz, length, C_HEADS, C_VAL_DIM).astype(jnp.float32))
    out = o.reshape(bsz, length, C_V_WIDTH).astype(h.dtype) @ w_out
    return out, (new_buf, s_new)

def run_trunk(x, past, norm_g, ffn_w_gate, ffn_w_up, ffn_w_down,
              ab_w_in, ab_b_f, ab_conv_w, ab_w_out,
              c_w_in, c_conv_w, c_a_log, c_dt_bias, c_norm_w, c_w_out):
    bsz = x.shape[0]
    ab_states, c_states = [], []
    for layer in range(DEPTH):
        gains = norm_g[layer]
        hdn = rmsnorm(x, gains[0])
        x = x + 0.5 * rmsnorm(swiglu(hdn, ffn_w_gate[layer, 0], ffn_w_up[layer, 0], ffn_w_down[layer, 0]), gains[1])
        hdn = rmsnorm(x, gains[2])
        i = layer // 2
        if layer % 2 == 0:
            if past is None:
                kvf = None
                buf = jnp.zeros((bsz, B_CONV - 1, B_WIDTH), x.dtype)
            else:
                cache_a_k, cache_a_v, cache_a_logf, page_table, state_b_conv, _, _ = past
                kvf = (gather_pages(cache_a_k, i, page_table),
                       gather_pages(cache_a_v, i, page_table),
                       gather_pages(cache_a_logf, i, page_table))
                buf = state_b_conv[i]
            mix, st = mixer_ab(hdn, ab_w_in[i], ab_b_f[i], ab_conv_w[i], ab_w_out[i], kvf, buf)
            ab_states.append(st)
        else:
            if past is None:
                buf = jnp.zeros((bsz, C_CONV - 1, C_CONV_WIDTH), x.dtype)
                s0 = jnp.zeros((bsz, C_HEADS, C_VAL_DIM, C_KEY_DIM), jnp.float32)
            else:
                _, _, _, _, _, state_c_conv, state_c_S = past
                buf = state_c_conv[i]
                s0 = state_c_S[i]
            mix, st = mixer_c(hdn, c_w_in[i], c_conv_w[i], c_a_log[i], c_dt_bias[i], c_norm_w[i], c_w_out[i], buf, s0)
            c_states.append(st)
        x = x + rmsnorm(mix, gains[3])
        hdn = rmsnorm(x, gains[4])
        x = x + 0.5 * rmsnorm(swiglu(hdn, ffn_w_gate[layer, 1], ffn_w_up[layer, 1], ffn_w_down[layer, 1]), gains[5])
    ab_new = [jnp.stack(t) for t in zip(*ab_states)]
    c_new = [jnp.stack(t) for t in zip(*c_states)]
    return x, ab_new, c_new

def setup_inputs(seed: int = 0) -> dict:
    key = jax.random.key(seed)
    ks = jax.random.split(key, 24)
    f32 = jnp.float32
    n_pages = PAST_LEN // PAGE_SIZE
    n_used = DEC_BATCH * n_pages
    n_phys = n_used + max(1, n_used // 4)

    def nrm(k, shape, scale):
        return jax.random.normal(k, shape, f32) * scale

    logf_shape = (N_AB_LAYERS, n_phys, PAGE_SIZE, A_HEADS)
    dt = jnp.exp(jax.random.uniform(ks[21], (N_C_LAYERS, C_HEADS), f32, float(np.log(DT_MIN)), float(np.log(DT_MAX))))
    return {
        'x_prompt': nrm(ks[0], (BATCH, SEQ, D_MODEL), 1.0),
        'x_sample': nrm(ks[1], (DEC_BATCH, DEC_SEQ, D_MODEL), 1.0),
        'cache_a_k': nrm(ks[2], (N_AB_LAYERS, n_phys, PAGE_SIZE, A_HEADS, A_HEAD_DIM), 1.0),
        'cache_a_v': nrm(ks[3], (N_AB_LAYERS, n_phys, PAGE_SIZE, A_HEADS, A_HEAD_DIM), 1.0),
        'cache_a_logf': jax.nn.log_sigmoid(jax.random.uniform(ks[4], logf_shape, f32, 1.0, 5.0) + nrm(ks[5], logf_shape, 0.5)),
        'page_table': jax.random.permutation(ks[6], n_phys)[:n_used].reshape(DEC_BATCH, n_pages).astype(jnp.int32),
        'state_b_conv': nrm(ks[7], (N_AB_LAYERS, DEC_BATCH, B_CONV - 1, B_WIDTH), 1.0),
        'state_c_conv': nrm(ks[8], (N_C_LAYERS, DEC_BATCH, C_CONV - 1, C_CONV_WIDTH), 1.0),
        'state_c_S': nrm(ks[9], (N_C_LAYERS, DEC_BATCH, C_HEADS, C_VAL_DIM, C_KEY_DIM), 0.1),
        'norm_g': 1.0 + nrm(ks[10], (DEPTH, 6, D_MODEL), 0.05),
        'ffn_w_gate': nrm(ks[11], (DEPTH, 2, D_MODEL, D_FF), D_MODEL ** -0.5),
        'ffn_w_up': nrm(ks[12], (DEPTH, 2, D_MODEL, D_FF), D_MODEL ** -0.5),
        'ffn_w_down': nrm(ks[13], (DEPTH, 2, D_FF, D_MODEL), D_FF ** -0.5),
        'ab_w_in': nrm(ks[14], (N_AB_LAYERS, D_MODEL, AB_IN_WIDTH), D_MODEL ** -0.5),
        'ab_b_f': jax.random.uniform(ks[15], (N_AB_LAYERS, A_HEADS), f32, 1.0, 5.0),
        'ab_conv_w': nrm(ks[16], (N_AB_LAYERS, B_CONV, B_WIDTH), B_CONV ** -0.5),
        'ab_w_out': nrm(ks[17], (N_AB_LAYERS, AB_OUT_WIDTH, D_MODEL), AB_OUT_WIDTH ** -0.5),
        'c_w_in': nrm(ks[18], (N_C_LAYERS, D_MODEL, C_IN_WIDTH), D_MODEL ** -0.5),
        'c_conv_w': nrm(ks[19], (N_C_LAYERS, C_CONV, C_CONV_WIDTH), C_CONV ** -0.5),
        'c_a_log': jnp.log(jax.random.uniform(ks[20], (N_C_LAYERS, C_HEADS), f32, 1.0, 16.0)),
        'c_dt_bias': dt + jnp.log(-jnp.expm1(-dt)),
        'c_norm_w': 1.0 + nrm(ks[22], (N_C_LAYERS, C_VAL_DIM), 0.05),
        'c_w_out': nrm(ks[23], (N_C_LAYERS, C_V_WIDTH, D_MODEL), C_V_WIDTH ** -0.5),
    }

def reference(x_prompt, x_sample, cache_a_k, cache_a_v, cache_a_logf, page_table,
              state_b_conv, state_c_conv, state_c_S,
              norm_g, ffn_w_gate, ffn_w_up, ffn_w_down,
              ab_w_in, ab_b_f, ab_conv_w, ab_w_out,
              c_w_in, c_conv_w, c_a_log, c_dt_bias, c_norm_w, c_w_out):
    y_prompt, ab_p, c_p = run_trunk(x_prompt, None, norm_g, ffn_w_gate, ffn_w_up, ffn_w_down,
                                    ab_w_in, ab_b_f, ab_conv_w, ab_w_out,
                                    c_w_in, c_conv_w, c_a_log, c_dt_bias, c_norm_w, c_w_out)
    past = (cache_a_k, cache_a_v, cache_a_logf, page_table, state_b_conv, state_c_conv, state_c_S)
    y_sample, ab_s, c_s = run_trunk(x_sample, past, norm_g, ffn_w_gate, ffn_w_up, ffn_w_down,
                                    ab_w_in, ab_b_f, ab_conv_w, ab_w_out,
                                    c_w_in, c_conv_w, c_a_log, c_dt_bias, c_norm_w, c_w_out)
    a_k_prompt, a_v_prompt, a_logf_prompt, b_conv_prompt = ab_p
    a_k_sample, a_v_sample, a_logf_sample, b_conv_sample = ab_s
    c_conv_prompt, c_S_prompt = c_p
    c_conv_sample, c_S_sample = c_s
    return (y_prompt, y_sample,
            a_k_prompt, a_v_prompt, a_logf_prompt,
            a_k_sample, a_v_sample, a_logf_sample,
            b_conv_prompt, b_conv_sample,
            c_conv_prompt, c_conv_sample,
            c_S_prompt, c_S_sample)


_drawn_inputs = setup_inputs


def setup_inputs(seed=0):
    import zlib

    import numpy as np

    out = dict(_drawn_inputs(seed))
    spreads = {}
    factors = {}
    for name, (base, spread) in spreads.items():
        noise = np.random.default_rng([zlib.crc32(name.encode()), seed]).standard_normal(out[name].shape)
        drawn = base * np.exp(spread * noise) if base else spread * noise
        out[name] = jnp.asarray(drawn.astype(out[name].dtype))
    for name, factor in factors.items():
        out[name] = (out[name] * factor).astype(out[name].dtype)
    return out
```

```python
from contextlib import ExitStack

import numpy as np

import concourse.bass as bass
from concourse import mybir
from concourse.alu_op_type import AluOpType as ALU

F32 = mybir.dt.float32
F32R = mybir.dt.float32r
I32 = mybir.dt.int32
ACT = mybir.ActivationFunctionType
AX = mybir.AxisListType

P = 128
D_MODEL = 1024
KD = D_MODEL // P
SEQ = 512
DEC_B = 8
DEC_S = 4
NS = DEC_B * DEC_S
T = SEQ + NS
TH = T // 2
PT = SEQ // P
D_FF = 2816
KF = D_FF // P
DEPTH = 2
EPS = 1e-6
KU = KF // 2
RAW = 4
MAGIC = 0x5F3759DF
A_HEADS = 8
A_DIM = 64
A_WIDTH = A_HEADS * A_DIM
NP = A_HEADS // 2
PAGE = 128
PAGES = 2048 // PAGE
B_WIDTH = D_MODEL // 2
B_CONV = 3
MB = B_WIDTH // P
NEG = -1e30
TINY = 1e-15
KR = 8
GP = 4
C_HEADS = 8
C_CONV = 4
GH = 4
LEVELS = 7

STAGES = {
    "tensor": (
        (
            "gains_psum",
        ),
        (
            "conv_b_psum", "page_offsets_psum", "cum_past_psum", "gates_psum", "b_tail_psum",
        ),
        (
            "hist_psum", "ba_psum", "tail_psum", "cum_psum",
        ),
    ),
    "scalar": (
        (),
        (
            "gate_exp", "gate_log", "b_tail_out",
        ),
        (
            "tail_rows", "c_gate_exp", "c_gate_log", "c_decays",
        ),
    ),
    "vector": (
        (
            "gains_ready",
        ),
        (
            "gate_abs", "gate_exp1", "page_totals", "pages_cumulated", "cumulated", "logf_rows_ready",
            "b_state_out", "gates_out", "b_tail_ready", "conv_b_done", "mixed_ready",
        ),
        (
            "hist_out", "c_gate_abs", "c_gate_exp1", "g_ready", "c_exponents", "cum_out",
        ),
    ),
    "gpsimd": (
        (
            "ident_zero", "ones_ready", "ident_ready",
        ),
        (
            "ab_zeros",
        ),
        (
            "c_constants_ready", "samples_staged",
        ),
    ),
}


PRIMED = 2
PRIMED_SEMS = ("hidden_ready", "attn_out", "probs_ready", "probs_turned", "probs_turned_psum", "pv_done", "kv_stored",
               "o_decode_ready", "tok_psum", "mixed_c", "o_normed", "final_stored", "final_psum")
SUBLAYERS = [("ffn", 0, 0), ("ab", 0, 0), ("ffn", 0, 1), ("ffn", 1, 0), ("c", 1, 0), ("ffn", 1, 1)]


def build(nc, io, subs=SUBLAYERS):
    stack = ExitStack()
    with stack:
        sems = {}

        def sem(name):
            if name not in sems:
                sems[name] = stack.enter_context(nc.semaphore(name))
            return sems[name]

        top = [0]

        nth = {}
        for both, even, odd in STAGES.values():
            names = both + even * (("ab", 0, 0) in subs) + odd * (("c", 1, 0) in subs)
            nth.update({name: n + 1 for n, name in enumerate(names)})
        passed = []

        def reached(name):
            engine = [x for x in STAGES if name in sum(STAGES[x], ())][0]
            passed.append(engine)
            assert passed.count(engine) == nth[name], name
            return 1

        def place(name, shape, dt, at=None):
            size = int(np.prod(shape[1:])) * 4
            off = top[0] if at is None else at
            if at is None:
                top[0] += (size + 31) // 32 * 32
            return nc.alloc_sbuf_tensor_at(name, shape, dt, offset=base + off), off

        base = nc.sbuf_base if not callable(nc.sbuf_base) else nc.sbuf_base()
        base = (base + 31) // 32 * 32

        xT, _ = place("xT", [P, KD, T], F32)
        hd_hi, at_hd = place("hd_hi", [P, KD, T], F32R)
        hd_lo, _ = place("hd_lo", [P, KD, T], F32R)
        h_hi, at_h = place("h_hi", [P, KF, T], F32R)
        h_lo, _ = place("h_lo", [P, KF, T], F32R)
        raw, _ = place("w_raw", [P, RAW, KU * P], F32)
        w_hi, _ = place("w_hi", [P, 2, KU * P], F32R)
        w_lo, _ = place("w_lo", [P, 2, KU * P], F32R)
        scr, _ = place("scratch", [P, 4, T], F32)
        ident, _ = place("ident", [P, P], F32)
        ones, _ = place("ones", [P, P], F32)
        gains, _ = place("gains", [P, DEPTH * 6 * KD], F32)
        rb, at_rb_free = place("rstd_rows", [P, T], F32)
        small, _ = place("small", [P, 64], F32)
        primer, _ = place("primer", [1, len(PRIMED_SEMS)], F32)
        y_ffn, _ = place("y_ffn", [P, KD, T], F32, at=at_hd)
        y_mix, _ = place("y_mix", [P, KD, T], F32, at=at_h)
        causal, _ = place("causal", [P, P], F32)
        before, _ = place("pages_before", [P, P], F32)
        same_b, _ = place("same_sample", [P, DEC_B], F32)
        new_mask, _ = place("new_key_mask", [NS, NS], F32)
        k_rows_s, at_krs = place("k_rows_sample", [NS, A_WIDTH], F32)
        small2, _ = place("c_small_2", [P, 104], F32)
        proj, _ = place("ab_proj", [P, 24, T], F32, at=at_h)
        at_free = [at_h + 24 * T * 4]

        def ab(name, shape, dt=F32, at=None):
            t, off = place(name, shape, dt, at=at_free[0] if at is None else at)
            if at is None:
                at_free[0] += (int(np.prod(shape[1:])) * 4 + 31) // 32 * 32
            return t, off

        aug_q, _ = ab("aug_q", [P, SEQ])
        aug_k, _ = ab("aug_k", [P, SEQ])
        q_st, at_qst = ab("q_staged", [P, T])
        k_st, at_kst = ab("k_staged", [P, T])
        v_st, at_vst = ab("v_staged", [P, T])
        k_rows, _ = ab("k_rows", [P, PT, P])
        v_rows, _ = ab("v_rows", [P, PT, P])
        probs, at_probs = ab("probs", [P, 2, SEQ])
        probs_t, at_probs_t = ab("probs_turned", [P, 2, SEQ])
        logf_t, _ = ab("logf_by_head", [A_HEADS, T])
        cum, _ = ab("cum_by_head", [A_HEADS, T])
        ck_past, _ = ab("cum_past", [P, A_HEADS, P])
        v_rows_s, _ = ab("v_rows_sample", [NS, A_WIDTH])
        k_new, _ = ab("k_new", [P, NP, NS])
        q_dec, _ = ab("q_decode", [P, NP, NS])
        cq_rows, _ = ab("cum_query_rows", [P, A_HEADS, NS])
        o_dec, _ = ab("o_decode", [P, DEC_B, NS])
        lf_rows, _ = ab("logf_rows", [P, PT + 1, A_HEADS])
        b_tail, _ = ab("b_tail", [P, MB, 2 + DEC_B * 2])
        assert at_free[0] <= at_h + 2 * KF * T * 4, at_free
        seg, _ = ab("segment_ones", [A_HEADS, T], at=at_vst)
        pages_f, _ = ab("logf_pages", [P, PAGE, A_HEADS], at=at_probs)
        pages_c, _ = ab("cum_pages", [P, A_HEADS, PAGE], at=at_probs_t)
        b_rows, _ = ab("b_state_rows", [DEC_B * 2, B_WIDTH], at=at_kst)
        bw_rows, _ = ab("b_weight_rows", [B_CONV * MB, P], at=at_qst)
        b_out_rows, _ = ab("b_out_rows", [2 + DEC_B * 2, B_WIDTH], at=at_kst)
        k_page, _ = ab("k_pages", [P, KR, A_WIDTH], at=at_h)
        v_page, _ = ab("v_pages", [P, PAGES, A_WIDTH], at=at_h + KR * A_WIDTH * 4)
        k_turned, _ = ab("k_turned", [P, 2, NP, GP * PAGE], at=at_h + (KR + PAGES) * A_WIDTH * 4)
        s_rows, _ = ab("s_rows", [NS, 2, GP * PAGE], at=at_probs)
        assert at_h + (KR + PAGES + 2 * GP) * A_WIDTH * 4 <= at_probs
        s_dec, _ = ab("s_decode", [P, PAGES, NS], at=at_probs_t)
        p_dec, _ = ab("p_decode", [P, PAGES, NS], at=at_probs_t + PAGES * NS * 4)
        pt_row, _ = place("page_row", [1, DEC_B * PAGES], I32)
        q_now = scr[:, 2, 0:160]
        q_diag = q_now.rearrange("p (q x) -> p q x", x=NS + 8)
        o_rows = scr[0:NS, 3, 0:A_WIDTH]
        tiny_ab, _ = place("ab_small", [P, 8 * NS + 128], F32)
        pt_col = tiny_ab[:, 0:1].bitcast(I32)
        b_f = tiny_ab[0:A_HEADS, 1:2]
        b_hist = tiny_ab[:, 8:8 + 64]
        b_w = tiny_ab[:, 72:72 + B_CONV * MB]
        ck_new = tiny_ab[0:NS, 88:96]
        page_tot = tiny_ab[:, 96:104]
        page_off = tiny_ab[:, 104:112]
        past_tot = tiny_ab[0:A_HEADS, 112:120]
        row_max = [tiny_ab[:, 120 + q:121 + q] for q in range(2)]
        row_sum = [tiny_ab[:, 122 + q:123 + q] for q in range(2)]
        row_inv = [tiny_ab[:, 124 + q:125 + q] for q in range(2)]
        mx_dec = tiny_ab[:, 128:160]
        sm_dec = tiny_ab[:, 160:192]
        inv_dec = tiny_ab[:, 192:224]
        s_new = tiny_ab[0:NS, 224:256]
        p_new = tiny_ab[0:NS, 256:288]
        dg_dec = tiny_ab[0:NS, 288:320]
        m_dec = tiny_ab[0:NS, 320:321]
        qkv, _ = place("c_qkv", [P, 24, T], F32, at=at_h)
        z_t, _ = place("c_z", [P, 8, T], F32, at=at_h + 24 * T * 4)
        at_free[0] = at_h + 32 * T * 4
        incl, _ = ab("incl", [P, P])
        later, _ = ab("later", [P, P])
        halves_m, _ = ab("half_masks", [P, LEVELS, P])
        incl_s, _ = ab("incl_sample", [NS, NS])
        same_s, _ = ab("same_sample_tokens", [NS, NS])
        own_s, _ = ab("own_tokens", [NS, DEC_B])
        c_w, _ = ab("c_conv_weights", [P, 96])
        s_all0, at_s0 = ab("states_0", [P, GH, DEC_B, P])
        stage_s, at_stage_s = ab("samples_staged", [P, 24, NS])
        assert at_free[0] <= at_h + 2 * KF * T * 4, at_free[0] - at_h
        hist_rows, _ = ab("c_state_rows", [24, 3072], at=at_s0)
        cw_rows, _ = ab("c_weight_rows", [96, P], at=at_s0 + 12288)
        conv_acc, _ = ab("conv_acc", [P, 2, 3 + SEQ + 7 * DEC_B], at=at_s0)
        tail, _ = ab("c_tail", [P, 24, 27], at=at_s0 + 4608)
        hist, _ = ab("c_history", [P, 24 * 24], at=at_s0 + 12800)
        s_all1, _ = ab("states_1", [P, GH, DEC_B, P], at=at_h)
        s_all = (s_all0, s_all1)
        s_turned, _ = ab("states_turned", [P, GH, DEC_B, P], at=at_h + 16384)
        kd_m, _ = ab("kd_masked", [NS, 2, DEC_B, P], at=at_h + 32768)
        kq_s, _ = ab("kq_sample", [P, 2, GH, NS], at=at_h + 40960)
        s_final, _ = ab("final_states", [P, GH, P], at=at_rb_free)
        tail_rows, _ = ab("tail_rows", [27, 3072], at=at_hd)
        slot = [at_hd]

        def quad(name, shape=None):
            t, _ = place(name, shape or [P, GH, P], F32, at=slot[0])
            slot[0] += int(np.prod((shape or [P, GH, P])[1:])) * 4
            return t

        stage = quad("stage", [P, 3, GH, P])
        kq_t = quad("kq_by_feature", [P, 2, GH, P])
        q_t, kb_t, tok_kd, tok_v, u_mat, p_t, state, u_vec, e_mat, x_m, x_t, t1 = (quad(x) for x in (
            "q_by_feature", "kb_by_feature", "kd_rows", "v_rows_c", "lower_turned", "qk_decay", "state", "u_vec",
            "decay", "x", "x_turned", "t1"))
        assert slot[0] <= at_hd + 2 * KD * T * 4
        b_mat = e_mat
        tok_q, tok_qd, tok_k = x_m, x_t, t1
        tok_kb = scr[:, 3, 0:GH * P].rearrange("p (h t) -> p h t", h=GH)
        ba_t, _ = ab("ba_by_feature", [P, T], at=at_stage_s)
        c_small, _ = place("c_small", [P, 512], F32, at=at_krs)
        at_small = [0]

        def take(n):
            at_small[0] += n
            assert at_small[0] <= 512
            return c_small[:, at_small[0] - n:at_small[0]]

        a_log, dt_bias, norm_w = take(8), take(8), take(1)
        take(3)
        gt = [take(40) for _ in range(4)]
        g_tok = take(40).rearrange("p (c h) -> p c h", h=8)
        beta, e_G, e_kd = take(40), take(40), take(40)
        e_last, e_last_s, nrm, nrm_r, nrm_t, fac = take(32), take(64), take(8), take(8), take(8), take(12)
        g_own, n_G = small2[:, 0:64], small2[:, 64:104]
        rows_p, _ = place("rows_prompt", [P, PT, D_MODEL], F32, at=at_h)
        rows_s, _ = place("rows_sample", [NS, D_MODEL], F32, at=at_h + PT * D_MODEL * 4)
        gain_rows, _ = place("gain_rows", [DEPTH * 6 * KD, P], F32, at=at_h + (PT + 1) * D_MODEL * 4)

        ps = stack.enter_context(nc.psum_tensor("ps", [P, 8, 512], F32))


        def cols(bank):
            return ps[:, bank:bank + 2, 0:TH]

        def halves(ap):
            return ap.rearrange("p (h t) -> p h t", h=2)

        gemms = {}
        order = []

        def gemm(name, kind, quads, nk, source, one_first=None):
            order.append(name)
            n0 = gemms[order[-2]]["end"] if len(order) > 1 else 0
            first = n0 + (1 if one_first is not None else 0)
            gemms[name] = dict(name=name, kind=kind, quads=quads, nk=nk, source=source, lead=one_first,
                               n0=n0, first=first, end=first + 4 * quads)

        def rows(w):
            return w.rearrange("(k p) n -> p k n", p=P)

        def ffn_sources(l, w):
            gate, up = rows(io["ffn_w_gate"][l, w]), rows(io["ffn_w_up"][l, w])
            down = rows(io["ffn_w_down"][l, w])
            gate_up = lambda i, j: (gate, up)[j % 2][:, :, bass.ds(i * (2 * P) + (j // 2) * P, P)]
            down_of = lambda i, j: down[:, (j % 2) * KU:(j % 2 + 1) * KU, bass.ds(i * (2 * P) + (j // 2) * P, P)]
            return gate_up, down_of

        def plain(w, at=0):
            w = rows(w)
            return lambda i, j: w[:, :, bass.ds(i * (4 * P) + (j * P + at), P)]

        ffns = [(l, w) for x, l, w in subs if x == "ffn"]
        for x, l, w in subs:
            if x == "ffn":
                gate_up, down_of = ffn_sources(l, w)
                gemm(f"gate_up{l}{w}", "gate_up", KF // 2, KD, gate_up)
                gemm(f"down{l}{w}", "down", KD // 2, KU, down_of)
            if x == "ab":
                w_in, w_out = io["ab_w_in"][0], io["ab_w_out"][0]
                gemm("ab_qkv", "proj", 3, KD, plain(w_in), one_first=rows(w_in)[:, :, 3 * A_WIDTH:3 * A_WIDTH + P])
                gemm("ab_gates", "proj", 3, KD, plain(w_in, 3 * A_WIDTH + A_HEADS))
                gemm("ab_out", "out", 2, KD, plain(w_out))
            if x == "c":
                w_in, w_out = io["c_w_in"][0], io["c_w_out"][0]
                gemm("c_qkv", "proj", 6, KD, plain(w_in), one_first=rows(w_in)[:, :, 4112 - P:4112])
                gemm("c_z", "proj", 2, KD, plain(w_in, 3072))
                gemm("c_out", "out", 2, KD, plain(w_out))

        def nk_of(n):
            for name in order:
                g = gemms[name]
                if g["n0"] <= n < g["end"]:
                    return g["nk"]
            return 0

        def sp_unit(e, g, i, j):
            n = g["first"] + j
            slot = n % RAW
            if n >= RAW or not isinstance(i, int):
                e.wait_ge(sem("w_lo_ready"), i * 4 + (n - RAW + 1))
            e.dma_start(raw[:, slot, 0:g["nk"] * P].rearrange("p (k n) -> p k n", n=P),
                        g["source"](i, j)).then_inc(sem(f"w_raw{slot}"), 16)

        def sp_gemm(e, g, only=None, after=0):
            start = after
            if g["lead"] is not None and not after:
                n = g["n0"]
                if n >= RAW:
                    e.wait_ge(sem("w_lo_ready"), n - RAW + 1)
                e.dma_start(raw[:, n % RAW, 0:KD * P].rearrange("p (k n) -> p k n", n=P),
                            g["lead"]).then_inc(sem(f"w_raw{n % RAW}"), 16)
            if only is not None:
                for i in only:
                    for j in range(4):
                        sp_unit(e, g, i, j)
                return
            if g["first"] < RAW and not after:
                for j in range(4):
                    sp_unit(e, g, 0, j)
                start = 1
            with e.Fori(start, g["quads"]) as i:
                for j in range(4):
                    sp_unit(e, g, i, j)

        def act_split(e, n, i, nk):
            if not nk:
                return
            e.wait_ge(sem(f"w_raw{n % RAW}"), i * 16 + 16 * (n // RAW + 1))
            if n >= 2:
                e.wait_ge(sem("unit_done"), i * 4 + (n - 1))
            e.copy(w_hi[:, n % 2, 0:nk * P], raw[:, n % RAW, 0:nk * P]).then_inc(sem("w_hi_ready"), 1)

        def dve_split(e, n, i, nk):
            if not nk:
                return
            e.wait_ge(sem("w_hi_ready"), i * 4 + (n + 1))
            e.tensor_tensor(w_lo[:, n % 2, 0:nk * P], raw[:, n % RAW, 0:nk * P],
                            w_hi[:, n % 2, 0:nk * P].bitcast(F32), ALU.subtract).then_inc(sem("w_lo_ready"), 1)

        hd_ready_by_chunk = [0]

        def pe_unit(e, n, i, nk, x_hi, x_lo, k0, bank, first, last, chunks=None):
            e.wait_ge(sem("w_lo_ready"), i * 4 + (n + 1))
            for k in range(nk):
                if chunks:
                    e.wait_ge(sem("hd_lo_ready"), chunks[0] + k + 1)
                wh, wl = (w[:, n % 2, k * P:(k + 1) * P] for w in (w_hi, w_lo))
                for w, x in ((wh, x_hi), (wh, x_lo), (wl, x_hi)):
                    for half in range(2):
                        mm = e.matmul(ps[:, bank + half, 0:TH], w, x[:, k0 + k, half * TH:(half + 1) * TH],
                                      start=first and k == 0 and w is wh and x is x_hi,
                                      stop=last and k == nk - 1 and w is wl)
            mm.then_inc(sem("unit_done"), 1)

        def quads(e, g, body, peel):
            n = g["quads"] - (1 if peel else 0)
            with e.Fori(0, n) as i:
                body(i, False)
            if peel:
                body(g["quads"] - 1, True)

        def gate_up_count(g):
            return KF * ffns.index((int(g["name"][-2]), int(g["name"][-1])))

        def pe_gate_up(e, g):
            m0 = gate_up_count(g)

            def body(i, lead):
                for j in range(4):
                    n = g["first"] + j
                    m = m0 + j // 2
                    if j % 2 == 0:
                        e.wait_ge(sem("hidden_ready"), i * 2 + (PRIMED + m - 1))
                    pe_unit(e, n, i, KD, hd_hi, hd_lo, 0, 4 * (m % 2) + 2 * (j % 2), True, True,
                            hd_ready_by_chunk if lead and j == 0 else None)

            body(0, True)
            with e.Fori(1, g["quads"]) as i:
                body(i, False)

        def act_gate_up(e, g):
            m0 = gate_up_count(g)
            e.preload_act_table(ACT.Silu)

            def body(i, last):
                for j in range(4):
                    n = g["first"] + j
                    act_split(e, n + 2, i, nk_of(n + 2 + 4 * (g["quads"] - 1)) if last else KD)
                    if j % 2:
                        m = m0 + j // 2
                        e.wait_ge(sem("unit_done"), i * 4 + (n + 1))
                        e.activation(halves(scr[:, m % 2, :]), cols(4 * (m % 2)), ACT.Silu).then_inc(sem("silu_ready"), 1)
                        e.wait_ge(sem("hidden_ready"), PRIMED + i * 2 + (m + 1))
                        e.copy(h_hi[:, bass.ds(i * 2 + j // 2, 1), :],
                               scr[:, 2 + m % 2:3 + m % 2, :]).then_inc(sem("h_hi_ready"), 1)

            quads(e, g, body, True)

        def dve_gate_up(e, g):
            m0 = gate_up_count(g)

            def body(i, last):
                for j in range(4):
                    n = g["first"] + j
                    dve_split(e, n + 2, i, nk_of(n + 2 + 4 * (g["quads"] - 1)) if last else KD)
                    if j % 2:
                        m = m0 + j // 2
                        e.wait_ge(sem("silu_ready"), i * 2 + (m + 1))
                        if m >= 2:
                            e.wait_ge(sem("h_lo_ready"), i * 2 + (m - 1))
                        e.tensor_tensor(halves(scr[:, 2 + m % 2, :]), halves(scr[:, m % 2, :]), cols(4 * (m % 2) + 2),
                                        ALU.mult).then_inc(sem("hidden_ready"), 1)
                        e.wait_ge(sem("h_hi_ready"), i * 2 + (m + 1))
                        e.tensor_tensor(h_lo[:, bass.ds(i * 2 + j // 2, 1), :], scr[:, 2 + m % 2:3 + m % 2, :],
                                        h_hi[:, bass.ds(i * 2 + j // 2, 1), :].bitcast(F32),
                                        ALU.subtract).then_inc(sem("h_lo_ready"), 1)

            quads(e, g, body, True)

        def proj_count(g):
            return 4 * sum(gemms[x]["quads"] for x in order[:order.index(g["name"])] if gemms[x]["kind"] == "proj")

        def pe_proj(e, g, after_lead=None):
            p0 = proj_count(g)
            if g["lead"] is not None:
                pe_unit(e, g["n0"], 0, KD, hd_hi, hd_lo, 0, 6, True, True, hd_ready_by_chunk)
            if after_lead:
                after_lead(e)

            def body(i, lead):
                for j in range(4):
                    if lead and g["lead"] is not None and j == 3:
                        e.wait_ge(sem("lead_ready"), 1 if g["name"] == "ab_qkv" else lead_c)
                    if not lead or p0:
                        e.wait_ge(sem("proj_ready"), i * 4 + (p0 + j - 3))
                    pe_unit(e, g["first"] + j, i, KD, hd_hi, hd_lo, 0, 2 * j, True, True)

            body(0, True)
            with e.Fori(1, g["quads"]) as i:
                body(i, False)

        lead_c = 1 + ("ab_qkv" in gemms)

        def act_proj(e, g, out, lead=None):
            if g["lead"] is not None:
                act_split(e, g["n0"] + 2, 0, KD)
                e.wait_ge(sem("unit_done"), g["n0"] + 1)
                lead(e)

            def body(i, last):
                for j in range(4):
                    n = g["first"] + j
                    act_split(e, n + 2, i, nk_of(n + 2 + 4 * (g["quads"] - 1)) if last else KD)
                    e.wait_ge(sem("unit_done"), i * 4 + (n + 1))
                    out(e, i, j)

            quads(e, g, body, True)

        def dve_proj(e, g, out=None):
            if g["lead"] is not None:
                dve_split(e, g["n0"] + 2, 0, KD)

            def body(i, last):
                for j in range(4):
                    n = g["first"] + j
                    dve_split(e, n + 2, i, nk_of(n + 2 + 4 * (g["quads"] - 1)) if last else KD)
                    if out:
                        out(e, i, j)

            quads(e, g, body, True)

        def y_count(g):
            return KD * [x for x in order if gemms[x]["kind"] in ("down", "out")].index(g["name"])

        def squares_to_psum(e, slot, first, last):
            for half in range(2):
                mm = e.matmul(ps[:, 6 + half, 0:TH], ones[:, :], scr[:, slot, half * TH:(half + 1) * TH],
                              start=first, stop=last, skip_group_check=True)
            mm.then_inc(sem("squares_summed"), 1)

        def pe_y(e, g, sq0):
            y0 = y_count(g)
            per = 2 if g["kind"] == "down" else 4
            x_hi, x_lo = (h_hi, h_lo) if g["kind"] == "down" else (hd_hi, hd_lo)

            def squares(i, t):
                e.wait_ge(sem("y_squared"), i * per + (y0 + t + 1))
                squares_to_psum(e, (y0 + t) % 2, isinstance(i, int) and i == 0 and t == 0, t < 0)

            def body(i, lead):
                for j in range(4):
                    n = g["first"] + j
                    t = j // 2 if per == 2 else j
                    bank = 2 * ((y0 + t) % 2)
                    opens = per == 4 or j % 2 == 0
                    if opens:
                        if g["kind"] == "down" and j == 0 and lead:
                            e.wait_ge(sem("h_lo_ready"), KF * (ffns.index((int(g["name"][-2]), int(g["name"][-1]))) + 1))
                        if not (lead and t < 2) or y0 + t >= 2:
                            e.wait_ge(sem("y_squared"), i * per + (y0 + t - 1))
                    pe_unit(e, n, i, g["nk"], x_hi, x_lo, (j % 2) * KU if per == 2 else 0, bank,
                            opens, per == 4 or j % 2 == 1)
                    if per == 4 or j % 2 == 1:
                        if not (lead and t == 0):
                            squares(i, t - 1)

            body(0, True)
            with e.Fori(1, g["quads"]) as i:
                body(i, False)
            squares(g["quads"], -1)

        def act_y(e, g, y):
            y0 = y_count(g)
            per = 2 if g["kind"] == "down" else 4

            def body(i, last):
                for j in range(4):
                    n = g["first"] + j
                    act_split(e, n + 2, i, nk_of(n + 2 + 4 * (g["quads"] - 1)) if last else g["nk"])
                    if per == 4 or j % 2:
                        t = j // 2 if per == 2 else j
                        m = y0 + t
                        e.wait_ge(sem("unit_done"), i * 4 + (n + 1))
                        e.copy(y[:, bass.ds(i * per + t, 1), :].rearrange("p o (h t) -> p (o h) t", h=2),
                               cols(2 * (m % 2))).then_inc(sem("y_ready"), 1)
                        e.wait_ge(sem("squares_summed"), i * per + (sq_base[g["name"]] + t - 1))
                        e.activation(halves(scr[:, m % 2, :]), cols(2 * (m % 2)),
                                     ACT.Square).then_inc(sem("y_squared"), 1)

            quads(e, g, body, True)

        def dve_y(e, g):
            def body(i, last):
                for j in range(4):
                    n = g["first"] + j
                    dve_split(e, n + 2, i, nk_of(n + 2 + 4 * (g["quads"] - 1)) if last else g["nk"])

            quads(e, g, body, True)

        sq_base = {}
        names_y = [x for x in order if gemms[x]["kind"] in ("down", "out")]
        for s, name in enumerate(names_y):
            sq_base[name] = KD * (2 * s + 1)

        def chain(e, ins):
            count["v"] += 1
            ins.then_inc(sem("vector_small"), 1)
            e.wait_ge(sem("vector_small"), count["v"])

        count = {"v": 0}

        def dve_norm(e, r):
            e.wait_ge(sem("squares_summed"), KD * (r + 1))
            mean, root, r_ = scr[:, 2, :], scr[:, 3, :], rb[:, :]
            e.tensor_scalar(halves(mean), cols(6), 1.0 / D_MODEL, EPS, ALU.mult, ALU.add).then_inc(sem("mean_ready"), 1)
            e.wait_ge(sem("root_ready"), r + 1)
            chain(e, e.reciprocal(r_, root))
            chain(e, e.tensor_tensor(root, r_, r_, ALU.mult))
            chain(e, e.scalar_tensor_tensor(root, root, -0.5, mean, ALU.mult, ALU.mult))
            chain(e, e.scalar_tensor_tensor(r_, root, 1.5, r_, ALU.add, ALU.mult))

        def act_norm(e, r):
            e.preload_act_table(ACT.Sqrt)
            e.wait_ge(sem("mean_ready"), r + 1)
            e.activation(scr[:, 3, :], scr[:, 2, :], ACT.Sqrt).then_inc(sem("root_ready"), 1)

        def gain(l, n, k):
            at = (l * 6 + n) * KD + k
            return gains[:, at:at + 1]

        def dve_pre(e, s, l, n):
            for k in range(KD + 1):
                if k < KD:
                    if k >= 2:
                        e.wait_ge(sem("hd_lo_ready"), s * KD + k - 1)
                    e.scalar_tensor_tensor(scr[:, k % 2, :], xT[:, k, :], gain(l, n, k), rb[:, :],
                                           ALU.mult, ALU.mult).then_inc(sem("hd_ready"), 1)
                if k >= 1:
                    e.wait_ge(sem("hd_hi_ready"), s * KD + k)
                    e.tensor_tensor(hd_lo[:, k - 1, :], scr[:, (k - 1) % 2, :], hd_hi[:, k - 1, :].bitcast(F32),
                                    ALU.subtract).then_inc(sem("hd_lo_ready"), 1)

        def act_pre(e, s):
            for k in range(KD):
                e.wait_ge(sem("hd_ready"), s * KD + k + 1)
                e.copy(hd_hi[:, k, :], scr[:, k % 2, :]).then_inc(sem("hd_hi_ready"), 1)

        def dve_post(e, s, l, n, y):
            for k in range(KD):
                e.wait_ge(sem("x_squared"), (s + 1) * KD + k - 1)
                e.scalar_tensor_tensor(scr[:, k % 2, :], y[:, k, :], gain(l, n, k), rb[:, :],
                                       ALU.mult, ALU.mult).then_inc(sem("branch_ready"), 1)
                e.wait_ge(sem("branch_ready"), s * KD + k + 1)
                e.tensor_tensor(xT[:, k, :], xT[:, k, :], scr[:, k % 2, :], ALU.add).then_inc(sem("x_ready"), 1)

        def act_squares_x(e, s):
            for k in range(KD):
                e.wait_ge(sem("x_ready"), s * KD + k + 1)
                if s or k >= 2:
                    e.wait_ge(sem("squares_summed"), 2 * s * KD + k - 1)
                e.activation(scr[:, 2 + k % 2, :], xT[:, k, :], ACT.Square).then_inc(sem("x_squared"), 1)

        def pe_squares_x(e, s):
            for k in range(KD):
                e.wait_ge(sem("x_squared"), s * KD + k + 1)
                squares_to_psum(e, 2 + k % 2, k == 0, k == KD - 1)

        def mark(e, name, ins):
            key = ("mark", name)
            count[key] = count.get(key, 0) + 1
            ins.then_inc(sem(name), 1)
            e.wait_ge(sem(name), count[key])

        def since(e, name, count):
            if not isinstance(count, int) or count > 0:
                e.wait_ge(sem(name), count)

        def pool_ab(e):
            def chained(ins):
                mark(e, "ab_constants", ins)

            def select(t, pattern, base, mult, fill, op=ALU.is_ge):
                chained(e.affine_select(out=t, in_=t, compare_op=op, fill=fill, base=base, pattern=pattern,
                                        channel_multiplier=mult))

            chained(e.memset(causal[:, :], 0.0))
            select(causal[:, :], [[-1, P]], 0, 1, NEG)
            chained(e.memset(before[:, :], 1.0))
            view = before[:, :].rearrange("p (b g) -> p b g", g=PAGES)
            select(view, [[-PAGES, DEC_B], [0, PAGES]], 0, 1, 0.0)
            select(view, [[PAGES, DEC_B], [1, PAGES]], -1, -1, 0.0)
            chained(e.memset(same_b[:, :], 1.0))
            select(same_b[:, :], [[-PAGES, DEC_B]], 0, 1, 0.0)
            select(same_b[:, :], [[PAGES, DEC_B]], PAGES - 1, -1, 0.0)
            chained(e.memset(new_mask[:, :], 0.0))
            view = new_mask[:, :].rearrange("p (b t) -> p b t", t=DEC_S)
            select(view, [[DEC_S, DEC_B], [1, DEC_S]], 0, -1, NEG)
            select(view, [[-DEC_S, DEC_B], [0, DEC_S]], 0, 1, NEG)
            e.wait_ge(sem("pages_in"), 32)
            if gemms["ab_qkv"]["n0"]:
                e.wait_ge(sem("unit_done"), gemms["ab_qkv"]["n0"])
            else:
                e.wait_ge(sem("x_ready"), KD)
            e.indirect_dma_start(pages_f[:, :, :].rearrange("p s h -> p (s h)"), None,
                                 io["cache_a_logf"].rearrange("l p s h -> (l p) (s h)"),
                                 bass.IndirectOffsetOnAxis(ap=pt_col.bitcast(mybir.dt.uint32), axis=0)
                                 ).then_inc(sem("logf_pages_in"), 16)
            chained(e.memset(seg[:, :], 1.0))
            chained(e.memset(seg[:, SEQ:T].rearrange("p (b t) -> p b t", t=DEC_S)[:, :, 0:1], 0.0))
            for t in (aug_q, aug_k):
                chained(e.memset(t[:, :], 0.0))
            for a in range(2):
                chained(e.memset(aug_q[64 * a:64 * a + A_HEADS, :], 1.0))
                chained(e.memset(aug_k[64 * a + 32:64 * a + 32 + A_HEADS, :], 1.0))
            e.memset(small[:, 63:64], 0.0).then_inc(sem("gpsimd_stage"), reached("ab_zeros"))

        def sp_ab(e):
            e.dma_start(pt_row[:, :], io["page_table"].rearrange("(o b) g -> o (b g)", o=1)).then_inc(sem("pages_in"), 16)
            e.dma_start(pt_col, io["page_table"].rearrange("b (g o) -> (b g) o", o=1)).then_inc(sem("pages_in"), 16)
            e.dma_start(b_f, io["ab_b_f"].rearrange("l h -> h l")).then_inc(sem("ab_small_in"), 16)
            sp_gemm(e, gemms["ab_qkv"], only=[0])
            if gemms["ab_qkv"]["n0"]:
                e.wait_ge(sem("unit_done"), gemms["ab_qkv"]["n0"])
            else:
                e.wait_ge(sem("x_ready"), KD)
            e.dma_start(b_rows[:, :], io["state_b_conv"][0].rearrange("b j d -> (b j) d")).then_inc(sem("ab_small_in"), 16)
            e.dma_start(bw_rows[:, :], io["ab_conv_w"][0].rearrange("j (m p) -> (j m) p", p=P)).then_inc(sem("ab_small_in"), 16)
            sp_gemm(e, gemms["ab_qkv"], after=1)
            sp_gemm(e, gemms["ab_gates"])
            sp_gemm(e, gemms["ab_out"], only=[0])
            e.wait_ge(sem("vector_stage"), nth["logf_rows_ready"])
            e.dma_start(io["a_logf_prompt"].rearrange("l b (c p) h -> p (l b c) h", p=P),
                        lf_rows[:, 0:PT, :]).then_inc(sem("stored"), 16)
            e.dma_start(io["a_logf_sample"].rearrange("l b t h -> (l b t) h"),
                        lf_rows[0:NS, PT, :]).then_inc(sem("stored"), 16)
            with e.Fori(0, NP) as i:
                e.wait_ge(sem("kv_rows"), i + 1)
                for name, t in (("a_k_prompt", k_rows), ("a_v_prompt", v_rows)):
                    dst = io[name].rearrange("l b (c p) h d -> p (l b c) (h d)", p=P)
                    e.dma_start(dst[:, :, bass.ts(i, P)], t[:, :, :]).then_inc(sem("kv_stored"), 16)
            for name, t in (("a_k_sample", k_rows_s), ("a_v_sample", v_rows_s)):
                e.dma_start(io[name].rearrange("l b t h d -> (l b t) (h d)"), t[:, :]).then_inc(sem("stored"), 16)
            k_cache = io["cache_a_k"].rearrange("l n s h d -> s (l n) (h d)")
            v_cache = io["cache_a_v"].rearrange("l n s h d -> s (l n) (h d)")
            last_page = k_cache.shape[1] - 1

            def load_key_page(b, g):
                page = e.value_load(pt_row[0:1, bass.ds(b * PAGES + g, 1)], min_val=0, max_val=last_page)
                since(e, "k_page_turned", b * PAGES + (g - KR + 1))
                e.dma_start(k_page[:, g % KR, :].rearrange("p (o n) -> p o n", o=1),
                            k_cache[:, bass.ds(page, 1), :]).then_inc(sem(f"k_page{g % KR // 2}"), 16)

            e.wait_ge(sem("staged"), NP)
            for g in range(KR):
                load_key_page(0, g)
            e.wait_ge(sem("vector_stage"), nth["conv_b_done"])
            e.dma_start(io["b_conv_prompt"].rearrange("l b j d -> (l b j) d"), b_out_rows[0:2, :]).then_inc(sem("stored"), 16)
            e.dma_start(io["b_conv_sample"].rearrange("l b j d -> (l b j) d"), b_out_rows[2:2 + 2 * DEC_B, :]
                        ).then_inc(sem("stored"), 16)
            def load_value_page(b, g):
                page = e.value_load(pt_row[0:1, bass.ds(b * PAGES + g, 1)], min_val=0, max_val=last_page)
                since(e, "v_page_used", b * PAGES + (g + 1 - PAGES))
                e.dma_start(v_page[:, g, :].rearrange("p (o n) -> p o n", o=1),
                            v_cache[:, bass.ds(page, 1), :]).then_inc(sem(f"v_page{g // 4}"), 16)

            def load_pages(b, another):
                for g in range(KR, PAGES):
                    load_key_page(b, g)
                if another:
                    for g in range(KR):
                        load_key_page(b + 1, g)
                for g in range(PAGES):
                    load_value_page(b, g)

            load_pages(0, True)
            with e.Fori(1, DEC_B - 1) as b:
                load_pages(b, True)
            load_pages(DEC_B - 1, False)
            sp_gemm(e, gemms["ab_out"], only=[1])

        def pe_ab(e):
            pe_proj(e, gemms["ab_qkv"])
            pe_proj(e, gemms["ab_gates"])
            e.wait_ge(sem("proj_ready"), proj_count(gemms["ab_gates"]) + 12)
            e.wait_ge(sem("ab_small_in"), 48)
            for m in range(MB):
                e.transpose(ps[:, 0, m * 16:(m + 1) * 16], b_rows[:, m * P:(m + 1) * P], ident[0:16, 0:16])
            n = B_CONV * MB
            e.transpose(ps[:, 0, 64:64 + n], bw_rows[:, :], ident[0:n, 0:n]).then_inc(sem("tensor_stage"), reached("conv_b_psum"))
            e.wait_ge(sem("vector_stage"), nth["page_totals"])
            e.matmul(ps[:, 1, 0:A_HEADS], before[:, :], page_tot, start=True, stop=True)
            e.matmul(ps[0:A_HEADS, 1, 8:8 + DEC_B], page_tot, same_b[:, :], start=True, stop=True
                     ).then_inc(sem("tensor_stage"), reached("page_offsets_psum"))
            e.wait_ge(sem("vector_stage"), nth["pages_cumulated"])
            for h in range(A_HEADS):
                mm = e.transpose(ps[:, 2 + h // 4, (h % 4) * P:(h % 4 + 1) * P], pages_c[:, h, :], ident[:, :])
            mm.then_inc(sem("tensor_stage"), reached("cum_past_psum"))
            e.wait_ge(sem("vector_stage"), nth["cumulated"])
            for c in range(PT + 1):
                n = P if c < PT else NS
                e.transpose(ps[0:n, 4, c * A_HEADS:(c + 1) * A_HEADS], logf_t[:, c * P:c * P + n],
                            ident[0:A_HEADS, 0:A_HEADS])
            e.transpose(ps[0:NS, 4, 40:48], cum[:, SEQ:T], ident[0:A_HEADS, 0:A_HEADS])
            e.matmul(ps[:, 5, 0:A_HEADS * NS], ones[0:A_HEADS, :], scr[0:A_HEADS, 3, 0:A_HEADS * NS],
                     start=True, stop=True).then_inc(sem("tensor_stage"), reached("gates_psum"))

            def scores(i, s):
                a, c = divmod(s, PT)
                if s == 0:
                    e.wait_ge(sem("staged"), i + 1)
                    e.wait_ge(sem("aug_ready"), i + 1)
                else:
                    e.wait_ge(sem("probs_ready"), PRIMED + i * 8 + (s - 1))
                n = (c + 1) * P
                out = ps[:, s % 2, 0:n]
                rows64 = slice(64 * a, 64 * a + 64)
                e.matmul(out, q_st[rows64, c * P:(c + 1) * P], k_st[rows64, 0:n], start=True, stop=False)
                e.matmul(out, aug_q[rows64, c * P:(c + 1) * P], aug_k[rows64, 0:n], start=False, stop=True
                         ).then_inc(sem("scores_ready"), 1)

            def turn(i, s):
                c = s % PT
                e.wait_ge(sem("probs_normed"), i * 8 + (s + 1))
                if s >= 1:
                    e.wait_ge(sem("probs_turned"), PRIMED + i * 8 + (s - 1))
                for k in range(c + 1):
                    mm = e.transpose(ps[:, 2 + s % 2, k * P:(k + 1) * P], probs[:, s % 2, k * P:(k + 1) * P], ident[:, :])
                mm.then_inc(sem("probs_turned_psum"), 1)

            def pv(i, s):
                a, c = divmod(s, PT)
                e.wait_ge(sem("probs_turned"), PRIMED + i * 8 + (s + 1))
                for k in range(c + 1):
                    mm = e.matmul(ps[64 * a:64 * a + 64, 4, c * P:(c + 1) * P], v_rows[:, k, 64 * a:64 * a + 64],
                                  probs_t[:, s % 2, k * P:(k + 1) * P], start=k == 0, stop=k == c)
                mm.then_inc(sem("pv_done"), 1)

            e.wait_ge(sem("vector_stage"), nth["gates_out"])
            with e.Fori(0, NP) as i:
                e.wait_ge(sem("attn_out"), PRIMED + i)
                e.wait_ge(sem("staged"), i + 1)
                for q, t in ((0, k_st), (1, v_st)):
                    for c in range(PT):
                        e.transpose(ps[:, 6 - q, c * P:(c + 1) * P], t[:, c * P:(c + 1) * P], ident[:, :])
                    mm = e.transpose(ps[0:NS, 7, q * P:(q + 1) * P], t[:, SEQ:T], ident[:, :])
                mm.then_inc(sem("kv_rows_psum"), 1)
                scores(i, 0)
                for s in range(8):
                    if s < 7:
                        scores(i, s + 1)
                    turn(i, s)
                    if s == 0:
                        e.wait_ge(sem("kv_rows"), i + 1)
                    if s >= 1:
                        pv(i, s - 1)
                pv(i, 7)

            e.wait_ge(sem("vector_stage"), nth["b_tail_ready"])
            for m in range(MB):
                mm = e.transpose(ps[0:2 + 2 * DEC_B, 0, m * P:(m + 1) * P], b_tail[:, m, :], ident[:, :])
            mm.then_inc(sem("tensor_stage"), reached("b_tail_psum"))
            e.wait_ge(sem("vector_stage"), nth["conv_b_done"])
            e.wait_ge(sem("attn_out"), PRIMED + NP)

            def page_turn(b, g):
                e.wait_ge(sem(f"k_page{g % KR // 2}"), b * 64 + 32 * (g // KR + 1))
                since(e, f"k_turned{g % 2}", b * 8 + g // 2)
                for q in range(NP):
                    mm = e.transpose(ps[:, g % 2, q * P:(q + 1) * P], k_page[:, g % KR, q * P:(q + 1) * P], ident[:, :])
                mm.then_inc(sem("k_page_turned"), 1)

            def group_scores(b, G):
                for x in range(2):
                    e.wait_ge(sem(f"k_turned{x}"), b * 8 + (G * 2 + 2))
                if G == 0:
                    e.wait_ge(sem("q_now_ready"), b + 1)
                since(e, "s_rows_ready", b * 4 + G)
                if G == 1:
                    since(e, "scores_out", b)
                for q in range(NP):
                    mm = e.matmul(ps[0:NS, 2 + 4 * (G % 2), :], q_now[:, q * NS:(q + 1) * NS], k_turned[:, G % 2, q, :],
                                  start=q == 0, stop=q == NP - 1)
                mm.then_inc(sem("group_scored"), 1)

            def group_turn(b, G):
                for x in range(GP):
                    at = (G * GP + x) * NS
                    mm = e.transpose(ps[:, 7, at:at + NS], s_rows[:, G % 2, x * PAGE:(x + 1) * PAGE], ident[0:NS, 0:NS])
                mm.then_inc(sem("group_turned"), 1)

            def all_scores(b, first=False):
                for G in range(PAGES // GP):
                    for x in range(GP):
                        page_turn(b, G * GP + x)
                    if G >= 1:
                        group_scores(b, G - 1)
                    if G >= 2:
                        group_turn(b, G - 2)
                group_scores(b, 3)
                group_turn(b, 2)
                e.wait_ge(sem("s_rows_ready"), b * 4 + 4)
                if first:
                    e.wait_ge(sem("o_decode_ready"), PRIMED)
                else:
                    e.wait_ge(sem("o_decode_ready"), PRIMED + b - 1)
                for q in range(NP):
                    mm = e.matmul(ps[0:NS, 3, q * 8:q * 8 + 8], k_new[:, q, :], q_now[:, q * 40:q * 40 + 8],
                                  start=True, stop=True)
                mm.then_inc(sem("new_scored"), 1)
                group_turn(b, 3)

            def maxima(b, first=False):
                e.wait_ge(sem("max_ready"), b + 1)
                e.transpose(ps[0:NS, 4, 0:P], mx_dec, ident[:, :]).then_inc(sem("max_turned"), 1)
                e.wait_ge(sem("max_diag"), b + 1)
                if not first:
                    e.wait_ge(sem("o_rows_ready"), b)
                e.matmul(ps[:, 4, P:P + NS], ones[0:NS, :], dg_dec, start=True, stop=True).then_inc(sem("max_rows"), 1)

            def weighted_values(b, last=False):
                e.wait_ge(sem("p_decode"), b + 1)
                e.wait_ge(sem("o_decode_ready"), PRIMED + b)
                for g in range(PAGES):
                    if g % 4 == 0:
                        e.wait_ge(sem(f"v_page{g // 4}"), b * 64 + 64)
                    e.matmul(ps[0:NS, 5, :], p_dec[:, g, :], v_page[:, g, :], start=g == 0, stop=False
                             ).then_inc(sem("v_page_used"), 1)
                e.matmul(ps[0:NS, 5, :], p_new, v_rows_s[:, :], start=False, stop=True)
                e.wait_ge(sem("sums_ready"), b + 1)
                e.wait_ge(sem("scores_out"), DEC_B if last else b + 2)
                e.matmul(ps[0:NS, 3, 200:201], sm_dec, ones[:, 0:1], start=True, stop=True).then_inc(sem("pv_decode"), 1)

            def turn_output(b):
                for q in range(NP):
                    mm = e.transpose(ps[:, 3, 256 + q * NS:256 + (q + 1) * NS], o_rows[:, q * P:(q + 1) * P],
                                     ident[0:NS, 0:NS])
                mm.then_inc(sem("o_turned"), 1)

            all_scores(0, True)
            maxima(0, True)
            with e.Fori(1, DEC_B) as b:
                all_scores(b)
                weighted_values(b - 1)
                maxima(b)
                turn_output(b - 1)
            weighted_values(DEC_B - 1, True)
            e.wait_ge(sem("o_rows_ready"), DEC_B)
            turn_output(DEC_B - 1)

            e.wait_ge(sem("vector_stage"), nth["mixed_ready"])
            pe_y(e, gemms["ab_out"], 0)

        def act_ab(e):
            def lead(e):
                e.copy(halves(scr[:, 0, :])[0:A_HEADS], cols(6)[0:A_HEADS]).then_inc(sem("lead_ready"), 1)

            def out_at(m0):
                def out(e, i, j):
                    e.copy(proj[:, bass.ds(i * 4 + (m0 + j), 1), :].rearrange("p o (h t) -> p (o h) t", h=2),
                           cols(2 * j)).then_inc(sem("proj_ready"), 1)
                return out

            act_proj(e, gemms["ab_qkv"], out_at(0), lead)
            act_proj(e, gemms["ab_gates"], out_at(12))
            e.preload_act_table_set("natural_log_exp_and_others")
            e.wait_ge(sem("vector_stage"), nth["gate_abs"])
            e.activation(scr[0:A_HEADS, 1, :], scr[0:A_HEADS, 1, :], ACT.Exp).then_inc(sem("scalar_stage"), reached("gate_exp"))
            e.wait_ge(sem("vector_stage"), nth["gate_exp1"])
            e.activation(scr[0:A_HEADS, 3, :], scr[0:A_HEADS, 2, :], ACT.Ln).then_inc(sem("scalar_stage"), reached("gate_log"))
            e.wait_ge(sem("gpsimd_stage"), nth["ab_zeros"])

            def exp(i, s):
                c = s % PT
                if s >= 1:
                    e.wait_ge(sem("probs_turned_psum"), PRIMED + i * 8 + (s - 1))
                e.wait_ge(sem("row_max"), i * 8 + (s + 1))
                n = (c + 1) * P
                e.activation(probs[:, s % 2, 0:n], ps[:, s % 2, 0:n], ACT.Exp, bias=row_max[s % 2],
                             accum_out=row_sum[s % 2]).then_inc(sem("probs_ready"), 1)

            def turned(i, s):
                c = s % PT
                e.wait_ge(sem("probs_turned_psum"), PRIMED + i * 8 + (s + 1))
                if s >= 1:
                    e.wait_ge(sem("pv_done"), PRIMED + i * 8 + (s - 1))
                n = (c + 1) * P
                e.copy(probs_t[:, s % 2, 0:n], ps[:, 2 + s % 2, 0:n]).then_inc(sem("probs_turned"), 1)

            with e.Fori(0, NP) as i:
                e.wait_ge(sem("vector_stage"), nth["b_state_out"])
                e.wait_ge(sem("attn_out"), PRIMED + i)
                e.activation(q_st[:, :], proj[:, bass.ds(i, 1), :].rearrange("p o t -> p (o t)"), ACT.Copy,
                             scale=A_DIM ** -0.5)
                e.copy(v_st[:, :], proj[:, bass.ds(i + 2 * NP, 1), :].rearrange("p o t -> p (o t)"))
                e.copy(k_st[:, :], proj[:, bass.ds(i + NP, 1), :].rearrange("p o t -> p (o t)")).then_inc(sem("staged"), 1)
                exp(i, 0)
                for s in range(1, 8):
                    exp(i, s)
                    turned(i, s - 1)
                turned(i, 7)
                e.wait_ge(sem("pv_done"), PRIMED + i * 8 + 8)
                e.copy(hd_hi[:, bass.ds(i, 1), 0:SEQ].rearrange("p o t -> p (o t)"), ps[:, 4, :]).then_inc(sem("attn_hi"), 1)

            e.wait_ge(sem("tensor_stage"), nth["b_tail_psum"])
            e.copy(b_out_rows[:, :], ps[0:2 + 2 * DEC_B, 0, :]).then_inc(sem("scalar_stage"), reached("b_tail_out"))

            e.wait_ge(sem("stored"), 16 * 6)
            e.wait_ge(sem("kv_stored"), PRIMED + 2 * 16 * NP)

            def exp_scores(b):
                def rows_out(G):
                    e.wait_ge(sem("group_scored"), b * 4 + (G + 1))
                    since(e, "group_turned", b * 4 + (G - 1))
                    e.copy(s_rows[:, G % 2, :], ps[0:NS, 2 + 4 * (G % 2), :]).then_inc(sem("s_rows_ready"), 1)

                for G in range(PAGES // GP):
                    since(e, "group_scored", b * 4 + (G - 1))
                    for g in (4 * G, 4 * G + 2):
                        e.wait_ge(sem("k_page_turned"), b * PAGES + (g + 1))
                        e.copy(k_turned[:, G % 2, :, (g % GP) * PAGE:(g % GP + 1) * PAGE],
                               ps[:, 0, :].rearrange("p (q n) -> p q n", n=PAGE)).then_inc(sem("k_turned0"), 1)
                    if G >= 1:
                        rows_out(G - 1)
                rows_out(3)
                e.wait_ge(sem("shifted"), b + 1)
                e.activation(p_new, s_new, ACT.Exp)
                e.activation(p_dec[:, :, :], s_dec[:, :, :], ACT.Exp).then_inc(sem("p_decode"), 1)

            exp_scores(0)
            with e.Fori(1, DEC_B) as b:
                exp_scores(b)

            e.wait_ge(sem("o_decode_ready"), PRIMED + DEC_B)
            for a in range(2):
                src = o_dec[64 * a:64 * a + 64, :, :].rearrange("p b (q a t) -> p a q b t", a=2, t=DEC_S)[:, a]
                for q in range(NP):
                    e.copy(hd_hi[64 * a:64 * a + 64, q, SEQ:T].rearrange("p (b t) -> p b t", t=DEC_S),
                           src[:, q]).then_inc(sem("sample_hi"), 1)
            act_y(e, gemms["ab_out"], y_mix)

        def dve_ab(e):
            dve_proj(e, gemms["ab_qkv"])
            dve_proj(e, gemms["ab_gates"])
            x, t1, t2, t3 = (scr[0:A_HEADS, q, :] for q in range(4))
            e.wait_ge(sem("lead_ready"), 1)
            e.wait_ge(sem("ab_small_in"), 48)
            chain(e, e.tensor_scalar(x, x, b_f, None, ALU.add))
            chain(e, e.tensor_scalar(t1, x, -1.0, None, ALU.mult))
            e.tensor_tensor(t1, t1, x, ALU.min).then_inc(sem("vector_stage"), reached("gate_abs"))
            e.wait_ge(sem("scalar_stage"), nth["gate_exp"])
            e.tensor_scalar(t2, t1, 1.0, None, ALU.add).then_inc(sem("vector_stage"), reached("gate_exp1"))
            e.wait_ge(sem("scalar_stage"), nth["gate_log"])
            chain(e, e.scalar_tensor_tensor(t3, t3, TINY, t1, ALU.add, ALU.mult))
            chain(e, e.tensor_scalar(t2, t2, -1.0, TINY, ALU.add, ALU.add))
            chain(e, e.reciprocal(t1, t2))
            chain(e, e.tensor_tensor(t3, t3, t1, ALU.mult))
            chain(e, e.scalar_tensor_tensor(logf_t[:, :], x, 0.0, t3, ALU.min, ALU.subtract))
            e.wait_ge(sem("gpsimd_stage"), nth["ab_zeros"])
            e.tensor_tensor_scan(cum[:, 0:SEQ], seg[:, 0:SEQ], logf_t[:, 0:SEQ], 0.0, ALU.mult, ALU.add)
            chain(e, e.tensor_tensor_scan(cum[:, SEQ:T], seg[:, SEQ:T], logf_t[:, SEQ:T], 0.0, ALU.mult, ALU.add))
            e.wait_ge(sem("logf_pages_in"), 16)
            for h in range(A_HEADS):
                ins = e.tensor_tensor_scan(pages_c[:, h, :], ones[:, :], pages_f[:, :, h], 0.0, ALU.mult, ALU.add)
            chain(e, ins)
            e.tensor_copy(page_tot, pages_c[:, :, PAGE - 1]).then_inc(sem("vector_stage"), reached("page_totals"))
            e.wait_ge(sem("tensor_stage"), nth["page_offsets_psum"])
            e.tensor_copy(page_off, ps[:, 1, 0:A_HEADS])
            chain(e, e.tensor_copy(past_tot, ps[0:A_HEADS, 1, 8:8 + DEC_B]))
            e.tensor_tensor(pages_c[:, :, :], pages_c[:, :, :], page_off.unsqueeze(2).to_broadcast([P, A_HEADS, PAGE]),
                            ALU.add).then_inc(sem("vector_stage"), reached("pages_cumulated"))
            view = cum[:, SEQ:T].rearrange("p (b t) -> p b t", t=DEC_S)
            chain(e, e.tensor_tensor(view, view, past_tot.unsqueeze(2).to_broadcast([A_HEADS, DEC_B, DEC_S]), ALU.add))
            e.tensor_tensor(scr[0:A_HEADS, 3, 0:A_HEADS * NS].rearrange("p (h t) -> p h t", t=NS),
                            cum[:, SEQ:T].unsqueeze(1).to_broadcast([A_HEADS, A_HEADS, NS]),
                            ident[0:A_HEADS, 0:A_HEADS].unsqueeze(2).to_broadcast([A_HEADS, A_HEADS, NS]),
                            ALU.mult).then_inc(sem("vector_stage"), reached("cumulated"))
            e.wait_ge(sem("tensor_stage"), nth["cum_past_psum"])
            e.tensor_copy(ck_past[:, :, :].rearrange("p (x y) k -> p x (y k)", x=2), ps[:, 2:4, :])
            e.wait_ge(sem("tensor_stage"), nth["gates_psum"])
            e.tensor_copy(lf_rows[:, 0:PT, :], ps[:, 4, 0:PT * A_HEADS].rearrange("p (c h) -> p c h", h=A_HEADS))
            e.tensor_copy(lf_rows[0:NS, PT, :], ps[0:NS, 4, PT * A_HEADS:(PT + 1) * A_HEADS]).then_inc(sem("vector_stage"), reached("logf_rows_ready"))
            e.tensor_copy(ck_new, ps[0:NS, 4, 40:48])
            e.wait_ge(sem("tensor_stage"), nth["conv_b_psum"])
            e.tensor_copy(b_hist, ps[:, 0, 0:64])
            e.tensor_copy(b_w, ps[:, 0, 64:64 + B_CONV * MB]).then_inc(sem("vector_stage"), reached("b_state_out"))
            e.tensor_copy(cq_rows[:, :, :], ps[:, 5, 0:A_HEADS * NS].rearrange("p (h t) -> p h t", t=NS)
                          ).then_inc(sem("vector_stage"), reached("gates_out"))

            def row_maxima(i, s):
                c = s % PT
                e.wait_ge(sem("scores_ready"), i * 8 + (s + 1))
                at = ps[:, s % 2, c * P:(c + 1) * P]
                e.tensor_tensor(at, at, causal[:, :], ALU.add).then_inc(sem("masked"), 1)
                e.wait_ge(sem("masked"), i * 8 + (s + 1))
                e.tensor_reduce(row_max[s % 2], ps[:, s % 2, 0:(c + 1) * P], AX.X, ALU.max,
                                negate=True).then_inc(sem("row_max"), 1)

            def normalise(i, s):
                c = s % PT
                e.wait_ge(sem("probs_ready"), PRIMED + i * 8 + (s + 1))
                e.reciprocal(row_inv[s % 2], row_sum[s % 2]).then_inc(sem("row_inv"), 1)
                e.wait_ge(sem("row_inv"), i * 8 + (s + 1))
                n = (c + 1) * P
                e.tensor_scalar(probs[:, s % 2, 0:n], probs[:, s % 2, 0:n], row_inv[s % 2], None,
                                ALU.mult).then_inc(sem("probs_normed"), 1)

            with e.Fori(0, NP) as i:
                e.wait_ge(sem("attn_out"), PRIMED + i)
                for a in range(2):
                    head = ident[0:A_HEADS, bass.ds(i * 2 + a, 1)]
                    e.tensor_scalar(aug_k[64 * a:64 * a + A_HEADS, :], cum[:, 0:SEQ], head, -1.0, ALU.mult, ALU.mult)
                    ins = e.tensor_scalar(aug_q[64 * a + 32:64 * a + 32 + A_HEADS, :], cum[:, 0:SEQ], head, None, ALU.mult)
                ins.then_inc(sem("aug_ready"), 1)
                e.wait_ge(sem("staged"), i + 1)
                e.tensor_copy(q_dec[:, bass.ds(i, 1), :].rearrange("p o t -> p (o t)"), q_st[:, SEQ:T])
                e.tensor_copy(k_new[:, bass.ds(i, 1), :].rearrange("p o t -> p (o t)"), k_st[:, SEQ:T])
                row_maxima(i, 0)
                e.wait_ge(sem("kv_rows_psum"), i + 1)
                e.wait_ge(sem("kv_stored"), PRIMED + i * 32)
                e.tensor_copy(k_rows[:, :, :].rearrange("p c n -> p (c n)"), ps[:, 6, :])
                e.tensor_copy(v_rows[:, :, :].rearrange("p c n -> p (c n)"), ps[:, 5, :])
                e.tensor_copy(k_rows_s[:, bass.ts(i, P)], ps[0:NS, 7, 0:P])
                e.tensor_copy(v_rows_s[:, bass.ts(i, P)], ps[0:NS, 7, P:2 * P]).then_inc(sem("kv_rows"), 1)
                for s in range(8):
                    if s < 7:
                        row_maxima(i, s + 1)
                    normalise(i, s)
                e.wait_ge(sem("attn_hi"), i + 1)
                e.tensor_tensor(hd_lo[:, bass.ds(i, 1), 0:SEQ].rearrange("p o t -> p (o t)"), ps[:, 4, :],
                                hd_hi[:, bass.ds(i, 1), 0:SEQ].rearrange("p o t -> p (o t)").bitcast(F32),
                                ALU.subtract).then_inc(sem("attn_out"), 1)

            EP, ES = 2 + SEQ, DEC_S + 2
            W = EP + DEC_B * ES - 2
            flat = scr[:, :, :].rearrange("p a t -> p (a t)")
            ext, acc = flat[:, 0:W + 2], flat[:, 2 * T:2 * T + W]
            e.wait_ge(sem("attn_out"), PRIMED + NP)
            for m in range(MB):
                es = ext[:, EP:EP + DEC_B * ES].rearrange("p (b t) -> p b t", t=ES)
                e.memset(ext[:, 0:2], 0.0)
                e.tensor_copy(es[:, :, 0:2], b_hist[:, m * 16:(m + 1) * 16].rearrange("p (b j) -> p b j", j=2))
                gc, u, gb = (proj[:, 12 + MB * q + m, :] for q in (1, 2, 0))
                e.tensor_tensor(ext[:, 2:EP], gc[:, 0:SEQ], u[:, 0:SEQ], ALU.mult)
                chain(e, e.tensor_tensor(es[:, :, 2:ES], gc[:, SEQ:T].rearrange("p (b t) -> p b t", t=DEC_S),
                                         u[:, SEQ:T].rearrange("p (b t) -> p b t", t=DEC_S), ALU.mult))
                e.tensor_copy(b_tail[:, m, 0:2], ext[:, SEQ:EP])
                e.tensor_copy(b_tail[:, m, 2:].rearrange("p (b j) -> p b j", j=2), es[:, :, DEC_S:ES])
                wj = lambda j: b_w[:, j * MB + m:j * MB + m + 1]
                chain(e, e.tensor_scalar(acc, ext[:, 0:W], wj(0), None, ALU.mult))
                for j in range(1, B_CONV):
                    chain(e, e.scalar_tensor_tensor(acc, ext[:, j:j + W], wj(j), acc, ALU.mult, ALU.add))
                e.tensor_tensor(gb[:, 0:SEQ], gb[:, 0:SEQ], acc[:, 0:SEQ], ALU.mult)
                gbs = gb[:, SEQ:T].rearrange("p (b t) -> p b t", t=DEC_S)
                padded = flat[:, 2 * T + EP:2 * T + EP + DEC_B * ES].rearrange("p (b t) -> p b t", t=ES)[:, :, 0:DEC_S]
                chain(e, e.tensor_tensor(gbs, gbs, padded, ALU.mult))
                chain(e, e.tensor_copy(hd_hi[:, MB + m, :], gb[:, :]))
                chain(e, e.tensor_tensor(hd_lo[:, MB + m, :], gb[:, :], hd_hi[:, MB + m, :].bitcast(F32), ALU.subtract))
            e.tensor_copy(small[:, 32:33], b_tail[:, 0, 0:1]).then_inc(sem("vector_stage"), reached("b_tail_ready"))
            e.wait_ge(sem("scalar_stage"), nth["b_tail_out"])
            e.tensor_copy(small[:, 33:34], hd_hi[:, MB, 0:1].bitcast(F32)).then_inc(sem("vector_stage"), reached("conv_b_done"))

            flat = scr[:, :, :].rearrange("p a t -> p (a t)")
            e.wait_ge(sem("stored"), 16 * 6)
            e.wait_ge(sem("kv_stored"), PRIMED + 2 * 16 * NP)
            chain(e, e.memset(q_now[:, :], 0.0))

            def output_rows(b):
                e.wait_ge(sem("pv_decode"), b + 1)
                e.reciprocal(inv_dec[0:NS, 0:1], ps[0:NS, 3, 200:201]).then_inc(sem("inv_ready"), 1)
                e.wait_ge(sem("inv_ready"), b + 1)
                e.tensor_scalar(o_rows[:, :], ps[0:NS, 5, :], inv_dec[0:NS, 0:1], None, ALU.mult).then_inc(sem("o_rows_ready"), 1)

            def output(b):
                e.wait_ge(sem("o_turned"), b + 1)
                for a in range(2):
                    at = slice(64 * a, 64 * a + 64)
                    ins = e.tensor_copy(
                        o_dec[at, bass.ds(b, 1), :].rearrange("p o (q a t) -> p (o q) a t", a=2, t=DEC_S)[:, :, a],
                        ps[at, 3, 256:256 + 160].rearrange("p (q x) -> p q x", x=40)[:, :, a * DEC_S:(a + 1) * DEC_S])
                ins.then_inc(sem("o_decode_ready"), 1)

            def softmax(b, first=False):
                since(e, "new_scored", b)
                for a in range(2):
                    at = slice(64 * a, 64 * a + 64)
                    e.tensor_copy(q_diag[at, :, a * DEC_S:(a + 1) * DEC_S], q_dec[at, :, bass.ds(b * DEC_S, DEC_S)]
                                  ).then_inc(sem("q_half"), 1)
                e.wait_ge(sem("q_half"), b * 2 + 2)
                e.tensor_copy(small[:, 30:31], q_now[:, 0:1]).then_inc(sem("q_now_ready"), 1)
                for G in range(PAGES // GP):
                    since(e, "group_scored", b * 4 + (G - 1))
                    for g in (4 * G + 1, 4 * G + 3):
                        e.wait_ge(sem("k_page_turned"), b * PAGES + (g + 1))
                        e.tensor_copy(k_turned[:, G % 2, :, (g % GP) * PAGE:(g % GP + 1) * PAGE],
                                      ps[:, 1, :].rearrange("p (q n) -> p q n", n=PAGE)).then_inc(sem("k_turned1"), 1)
                step = [0]
                per = 6

                def own(ins):
                    step[0] += 1
                    ins.then_inc(sem("decode_step"), 1)
                    e.wait_ge(sem("decode_step"), b * per + step[0])

                e.wait_ge(sem("new_scored"), b + 1)
                e.wait_ge(sem("group_turned"), b * 4 + 4)
                by_head = lambda t: t.rearrange("p g (h t) -> p g h t", t=DEC_S)
                ck = ck_past[:, :, bass.ds(b * PAGES, PAGES)].rearrange("p h g -> p g h")
                cq = cq_rows[:, :, bass.ds(b * DEC_S, DEC_S)]
                sn = s_new.rearrange("p (h t) -> p h t", t=DEC_S)
                e.tensor_tensor(by_head(s_dec[:, :, :]), by_head(ps[:, 7, :].rearrange("p (g n) -> p g n", n=NS)),
                                ck.unsqueeze(3).to_broadcast([P, PAGES, A_HEADS, DEC_S]), ALU.subtract)
                own(e.tensor_tensor(sn, ps[0:NS, 3, 0:NS].rearrange("p (h t) -> p h t", t=DEC_S),
                                    ck_new.unsqueeze(2).to_broadcast([NS, A_HEADS, DEC_S]), ALU.subtract))
                e.tensor_tensor(by_head(s_dec[:, :, :]), by_head(s_dec[:, :, :]),
                                cq.unsqueeze(1).to_broadcast([P, PAGES, A_HEADS, DEC_S]), ALU.add).then_inc(sem("scores_out"), 1)
                own(e.tensor_tensor(sn, sn, cq[0:NS], ALU.add))
                own(e.tensor_tensor(sn, sn, new_mask[:, bass.ds(b * DEC_S, DEC_S)].unsqueeze(1).to_broadcast(
                    [NS, A_HEADS, DEC_S]), ALU.add))
                own(e.tensor_reduce(mx_dec, s_dec[:, :, :].rearrange("p g n -> p n g"), AX.X, ALU.max))
                e.tensor_tensor(mx_dec[0:NS], mx_dec[0:NS], s_new, ALU.max).then_inc(sem("max_ready"), 1)
                if not first:
                    output_rows(b - 1)
                e.wait_ge(sem("max_turned"), b + 1)
                own(e.tensor_reduce(m_dec, ps[0:NS, 4, 0:P], AX.X, ALU.max))
                e.tensor_scalar(dg_dec, ident[0:NS, 0:NS], m_dec, None, ALU.mult).then_inc(sem("max_diag"), 1)
                e.wait_ge(sem("max_rows"), b + 1)
                rows_max = ps[:, 4, P:P + NS]
                e.tensor_tensor(s_new, s_new, rows_max[0:NS], ALU.subtract)
                e.tensor_tensor(s_dec[:, :, :], s_dec[:, :, :], rows_max.unsqueeze(1).to_broadcast([P, PAGES, NS]),
                                ALU.subtract).then_inc(sem("shifted"), 1)
                if not first:
                    output(b - 1)
                e.wait_ge(sem("p_decode"), b + 1)
                own(e.tensor_reduce(sm_dec, p_dec[:, :, :].rearrange("p g n -> p n g"), AX.X, ALU.add))
                e.tensor_tensor(sm_dec[0:NS], sm_dec[0:NS], p_new, ALU.add).then_inc(sem("sums_ready"), 1)

            softmax(0, True)
            with e.Fori(1, DEC_B) as b:
                softmax(b)
            output_rows(DEC_B - 1)
            output(DEC_B - 1)

            e.wait_ge(sem("sample_hi"), 8)
            for a in range(2):
                src = o_dec[64 * a:64 * a + 64, :, :].rearrange("p b (q a t) -> p a q b t", a=2, t=DEC_S)[:, a]
                for q in range(NP):
                    at = (slice(64 * a, 64 * a + 64), q, slice(SEQ, T))
                    ins = e.tensor_tensor(hd_lo[at].rearrange("p (b t) -> p b t", t=DEC_S), src[:, q],
                                          hd_hi[at].bitcast(F32).rearrange("p (b t) -> p b t", t=DEC_S), ALU.subtract)
            ins.then_inc(sem("vector_stage"), reached("mixed_ready"))
            dve_y(e, gemms["ab_out"])


        def pool_c(e):
            def chained(ins):
                mark(e, "c_constants", ins)

            def select(t, pattern, base, mult, fill, op=ALU.is_ge):
                chained(e.affine_select(out=t, in_=t, compare_op=op, fill=fill, base=base, pattern=pattern,
                                        channel_multiplier=mult))

            if gemms["c_qkv"]["n0"]:
                e.wait_ge(sem("unit_done"), gemms["c_qkv"]["n0"])
            else:
                e.wait_ge(sem("x_ready"), KD)
            if ("ab", 0, 0) in subs:
                e.wait_ge(sem("vector_stage"), nth["mixed_ready"])
            for t in (incl, later, incl_s):
                chained(e.memset(t[:, :], 1.0))
            chained(e.memset(halves_m[:, :, :], 1.0))
            chained(e.memset(own_s[:, :], 1.0))
            chained(e.memset(same_s[:, :], 1.0))
            select(incl[:, :], [[1, P]], 0, -1, 0.0)
            select(later[:, :], [[-1, P]], -1, 1, 0.0)
            view = same_s[:, :].rearrange("p (b t) -> p b t", t=DEC_S)
            select(view, [[-DEC_S, DEC_B], [0, DEC_S]], 0, 1, 0.0)
            select(view, [[DEC_S, DEC_B], [0, DEC_S]], DEC_S - 1, -1, 0.0)
            select(own_s[:, :], [[-DEC_S, DEC_B]], 0, 1, 0.0)
            select(own_s[:, :], [[DEC_S, DEC_B]], DEC_S - 1, -1, 0.0)
            chained(e.tensor_tensor(incl_s[:, :], same_s[:, :], incl[0:NS, 0:NS], ALU.mult))
            for l in range(LEVELS):
                size = 2 ** (l + 1)
                view = halves_m[:, l, :].rearrange("p (b x) -> p b x", x=size)
                select(view, [[-size, P // size], [0, size]], 0, 1, 0.0)
                select(view, [[size, P // size], [0, size]], size // 2 - 1, -1, 0.0)
                if l:
                    chained(e.memset(view[:, :, 0:size // 2], 0.0))
                else:
                    chained(e.memset(view[:, :, 0:1], 0.0))
            chained(e.memset(c_small[:, :], 0.0))
            e.memset(c_small[:, 500:501], 0.0).then_inc(sem("gpsimd_stage"), reached("c_constants_ready"))

            e.wait_ge(sem("tail_stored"), 32)
            e.wait_ge(sem("conv_ready"), 24)
            e.wait_ge(sem("tensor_stage"), nth["ba_psum"])
            e.tensor_copy(stage_s[:, :, :], qkv[:, :, SEQ:T]).then_inc(sem("gpsimd_stage"), reached("samples_staged"))
            with e.Fori(0, 2) as gp:
                with e.Fori(0, PT) as c:
                    pool_chunk(e, gp, c, gp * PT + c, "")
            for gp in range(2):
                pool_chunk(e, gp, None, gp, "_s")

        PER_CHUNK = {"t1_psum": 2 * LEVELS - 2, "t1_ready": 2 * LEVELS - 2, "x_step_psum": 2 * LEVELS - 2,
                     "x_step": 2 * LEVELS - 2, "mt_ready": LEVELS - 1, "chunk_step": 32}

        def chunks_before(name, sfx):
            return (PRIMED if name in PRIMED_SEMS else 0) + (2 * PT * PER_CHUNK.get(name, 1) if sfx else 0)

        def levels_of(sfx):
            return 2 if sfx else LEVELS

        def pool_chunk(e, gp, c, it, sfx):
            n = NS if sfx else P
            if not sfx:
                e.wait_ge(sem("tok_psum"), PRIMED + it)
                for x in range(3):
                    src = qkv[:, bass.ds(gp * GH + 2 * GH * x, GH), bass.ds(c * P, P)]
                    ins = e.tensor_copy(stage[:, x, :, :], src)
                ins.then_inc(sem("staged_c"), 1)
            e.wait_ge(sem("kk_out"), chunks_before("kk_out", sfx) + it + 1)
            per = levels_of(sfx) - 1
            for l in range(1, levels_of(sfx)):
                if l >= 3:
                    e.wait_ge(sem("t1_psum"), chunks_before("t1_psum", sfx) + it * 2 * per + 2 * (l - 2))
                e.tensor_tensor(mt(l)[0:n, :, 0:n], u_mat[0:n, :, 0:n],
                                halves_m[0:n, l, 0:n].unsqueeze(1).to_broadcast([n, GH, n]),
                                ALU.mult).then_inc(sem("mt_ready"), 1)

        def mt(l):
            return scr[:, 2 + l % 2, 0:GH * P].rearrange("p (h t) -> p h t", h=GH)

        def sp_c(e):
            sp_gemm(e, gemms["c_qkv"], only=[0])
            if gemms["c_qkv"]["n0"]:
                e.wait_ge(sem("unit_done"), gemms["c_qkv"]["n0"])
            else:
                e.wait_ge(sem("x_ready"), KD)
            e.dma_start(hist_rows[:, :], io["state_c_conv"][0].rearrange("b j d -> (b j) d")).then_inc(sem("c_rows_in"), 16)
            e.dma_start(cw_rows[:, :], io["c_conv_w"][0].rearrange("j (m p) -> (j m) p", p=P)).then_inc(sem("c_rows_in"), 16)
            e.wait_ge(sem("gpsimd_stage"), nth["c_constants_ready"])
            e.dma_start(a_log, io["c_a_log"][0:1, :].to_broadcast([P, C_HEADS])).then_inc(sem("c_small_in"), 16)
            e.dma_start(dt_bias, io["c_dt_bias"][0:1, :].to_broadcast([P, C_HEADS])).then_inc(sem("c_small_in"), 16)
            e.dma_start(norm_w, io["c_norm_w"].rearrange("l d -> d l")).then_inc(sem("c_small_in"), 16)
            sp_gemm(e, gemms["c_qkv"], after=1)
            sp_gemm(e, gemms["c_z"])
            sp_gemm(e, gemms["c_out"], only=[0])
            e.wait_ge(sem("scalar_stage"), nth["tail_rows"])
            e.dma_start(io["c_conv_prompt"].rearrange("l b j d -> (l b j) d"), tail_rows[0:3, :]).then_inc(sem("tail_stored"), 16)
            e.dma_start(io["c_conv_sample"].rearrange("l b j d -> (l b j) d"), tail_rows[3:27, :]).then_inc(sem("tail_stored"), 16)
            e.wait_ge(sem("tail_stored"), 32)
            s_in = io["state_c_S"][0].rearrange("b h v k -> v h b k")
            s_out = io["c_S_sample"][0].rearrange("b h v k -> v h b k")
            e.wait_ge(sem("gpsimd_stage"), nth["samples_staged"])
            for j in range(GH):
                e.dma_start(s_all[0][:, j], s_in[:, j]).then_inc(sem("states_in0"), 16)
            for gp in range(2):
                e.wait_ge(sem("final_state"), gp + 1)
                e.dma_start(io["c_S_prompt"][0, 0].rearrange("h v k -> v h k")[:, gp * GH:(gp + 1) * GH, :],
                            s_final[:, :, :]).then_inc(sem("final_stored"), 16)
            e.wait_ge(sem("final_stored"), PRIMED + 32)
            for j in range(GH):
                e.dma_start(s_all[1][:, j], s_in[:, GH + j]).then_inc(sem("states_in1"), 16)
            for gp in range(2):
                e.wait_ge(sem("states_out"), gp + 1)
                for j in range(GH):
                    e.dma_start(s_out[:, gp * GH + j], s_all[gp][:, j]).then_inc(sem("states_stored"), 16)
            e.wait_ge(sem("states_stored"), 16 * 8)
            sp_gemm(e, gemms["c_out"], only=[1])

        def pe_c_first(e):
            e.wait_ge(sem("c_rows_in"), 32)
            for m in range(24):
                e.transpose(ps[:, 4 + m // 12, (m % 12) * 24:(m % 12 + 1) * 24], hist_rows[:, m * P:(m + 1) * P], ident[0:24, 0:24])
            e.transpose(ps[:, 2, 0:96], cw_rows[:, :], ident[0:96, 0:96]).then_inc(sem("tensor_stage"), reached("hist_psum"))
            e.wait_ge(sem("vector_stage"), nth["hist_out"])

        def pe_chunk(e, gp, it, sfx):
            n = NS if sfx else P
            per = levels_of(sfx) - 1

            def wait(name, k=1, each=1):
                e.wait_ge(sem(name), chunks_before(name, sfx) + it * each + k)

            src = (lambda x, j: stage_s[:, x * 8 + it * GH + j, :]) if sfx else (lambda x, j: stage[:, x, j, :])
            wait("o_normed", 0)
            if sfx:
                e.wait_ge(sem("final_state"), 2)
            else:
                wait("staged_c")
            for bank, x in ((0, 2), (1, 1), (2, 0)):
                for j in range(GH):
                    mm = e.transpose(ps[0:n, bank, j * P:(j + 1) * P], src(x, j), ident[:, :])
            mm.then_inc(sem("tok_psum"), 1)
            wait("g_masked")
            e.matmul(ps[0:n, 7, 0:GH * n], later[0:n, 0:n], scr[0:n, 1, 0:GH * n],
                     start=True, stop=True).then_inc(sem("decay_psum"), 1)
            wait("tok_scaled")
            for bank, t in ((3, tok_k), (4, tok_qd), (5, tok_q), (6, tok_kb)):
                for j in range(GH):
                    mm = e.transpose(ps[:, bank, j * n:(j + 1) * n], t[0:n, j, :], ident[0:n, 0:n])
            mm.then_inc(sem("feat_psum"), 1)
            wait("feat_ready")
            wait("feat_b_ready")
            for bank, t in ((0, kb_t), (1, q_t)):
                for j in range(GH):
                    mm = e.matmul(ps[0:n, bank, j * n:(j + 1) * n], kq_t[:, 0, j, 0:n], t[:, j, 0:n], start=True, stop=True)
            mm.then_inc(sem("kk_psum"), 1)
            wait("kk_out")
            if not sfx:
                e.wait_ge(sem("state_ready"), it + (gp + 1))
                for j in range(GH):
                    mm = e.matmul(ps[:, 0, j * P:(j + 1) * P], kq_t[:, 0, j, :], state[:, j, :], start=True, stop=True)
                mm.then_inc(sem("kr_psum"), 1)
            else:
                e.wait_ge(sem(f"states_in{it}"), 64)
                for j in range(GH):
                    if j >= 2:
                        e.wait_ge(sem("turned_a"), it * GH + j - 1)
                        e.wait_ge(sem("turned_b"), it * GH + j - 1)
                    for b in range(DEC_B):
                        mm = e.transpose(ps[:, 4 + 2 * (j % 2) + b // 4, (b % 4) * P:(b % 4 + 1) * P],
                                         s_all[it][:, j, b, :], ident[:, :])
                    mm.then_inc(sem("states_psum"), 1)
                e.wait_ge(sem("turned_a"), it * GH + GH)
                e.wait_ge(sem("turned_b"), it * GH + GH)
                kq_out = ps[:, 0, 0:2 * GH * NS].rearrange("p (x j t) -> p x j t", x=2, j=GH)
                for j in range(GH):
                    for b in range(DEC_B):
                        at = slice(b * DEC_S, (b + 1) * DEC_S)
                        mm = e.matmul(kq_out[:, :, j, at], s_turned[:, j, b, :], kq_t[:, :, j, at], start=True, stop=True)
                mm.then_inc(sem("kq_psum"), 1)
                e.wait_ge(sem("kq_ready"), it + 1)
                for j in range(GH):
                    mm = e.transpose(ps[0:n, 3, j * P:(j + 1) * P], kq_s[:, 0, j, :], ident[:, :])
                mm.then_inc(sem("kr_psum"), 1)
                wait("b_ready")
            wait("xt1_ready")
            for j in range(GH):
                mm = e.transpose(ps[0:n, 2, j * n:(j + 1) * n], x_t[0:n, j, 0:n], ident[0:n, 0:n])
            mm.then_inc(sem("x0_psum"), 1)
            wait("x0_ready")
            for l in range(1, levels_of(sfx)):
                wait("mt_ready", l, per)
                for hf in range(2):
                    if l > 1:
                        wait("x_step", 2 * (l - 2) + hf + 1, 2 * per)
                    for j in (2 * hf, 2 * hf + 1):
                        mm = e.matmul(ps[0:n, 2 + hf, j * n:(j + 1) * n], mt(l)[0:n, j, 0:n], x_m[0:n, j, 0:n],
                                      start=True, stop=True)
                    mm.then_inc(sem("t1_psum"), 1)
                for hf in range(2):
                    wait("t1_ready", 2 * (l - 1) + hf + 1, 2 * per)
                    for j in (2 * hf, 2 * hf + 1):
                        if l < per:
                            e.matmul(ps[0:n, 4 + hf, j * n:(j + 1) * n], x_t[0:n, j, 0:n], t1[0:n, j, 0:n],
                                     start=True, stop=True)
                        mm = e.matmul(ps[0:n, 6 + hf, j * n:(j + 1) * n], t1[0:n, j, 0:n], x_t[0:n, j, 0:n],
                                      start=True, stop=True)
                    mm.then_inc(sem("x_step_psum"), 1)
            wait("b_ready")
            wait("xb_ready")
            for j in range(GH):
                mm = e.matmul(ps[0:n, 1, j * P:(j + 1) * P], x_t[0:n, j, 0:n], b_mat[0:n, j, :], start=True, stop=True)
            mm.then_inc(sem("u_psum"), 1)
            wait("u_ready")
            for j in range(GH):
                out = ps[0:n, 2, j * P:(j + 1) * P]
                if sfx:
                    e.matmul(out, kq_s[:, 1, j, :], ident[:, :], start=True, stop=False)
                else:
                    e.matmul(out, kq_t[:, 1, j, :], state[:, j, :], start=True, stop=False)
                mm = e.matmul(out, p_t[0:n, j, 0:n], u_vec[0:n, j, :], start=False, stop=True)
            mm.then_inc(sem("o_psum"), 1)
            if not sfx:
                for j in range(GH):
                    mm = e.matmul(ps[:, 3, j * P:(j + 1) * P], tok_kd[:, j, :], u_vec[:, j, :], start=True, stop=True)
                mm.then_inc(sem("dr_psum"), 1)
            else:
                for j in range(GH):
                    e.wait_ge(sem("kd_masked"), it * GH + j + 1)
                    if j:
                        e.wait_ge(sem("state_step"), it * GH + j)
                    for x in range(2):
                        mm = e.matmul(ps[:, 6 + x, :], u_vec[0:n, j, :],
                                      kd_m[0:n, j % 2, 4 * x:4 * x + 4, :].rearrange("p b k -> p (b k)"), start=True, stop=True)
                    mm.then_inc(sem("ds_psum"), 1)
            wait("o_normed")
            for j in range(GH):
                mm = e.transpose(ps[:, 4, j * n:(j + 1) * n], t1[0:n, j, :], ident[0:n, 0:n])
            mm.then_inc(sem("ot_psum"), 1)

        def pe_c(e):
            pe_proj(e, gemms["c_qkv"], pe_c_first)
            pe_proj(e, gemms["c_z"])
            e.wait_ge(sem("proj_ready"), proj_count(gemms["c_z"]) + 8)
            for c in range(PT):
                e.transpose(ps[:, 0, c * P:(c + 1) * P], ba_t[:, c * P:(c + 1) * P], ident[:, :])
            e.transpose(ps[0:NS, 1, 0:P], ba_t[:, SEQ:T], ident[:, :]).then_inc(sem("tensor_stage"), reached("ba_psum"))
            e.wait_ge(sem("conv_acc"), 24)
            for m in range(24):
                mm = e.transpose(ps[0:27, 2 + m // 4, (m % 4) * P:(m % 4 + 1) * P], tail[:, m, :], ident[:, :])
            mm.then_inc(sem("tensor_stage"), reached("tail_psum"))
            e.wait_ge(sem("vector_stage"), nth["g_ready"])
            g32 = g_tok[:, 0:PT, :].rearrange("p c h -> p (c h)")
            e.matmul(ps[:, 0, 0:32], incl[:, :], g32, start=True, stop=True)
            e.matmul(ps[:, 0, 32:64], ones[:, :], g32, start=True, stop=True)
            e.matmul(ps[0:NS, 1, 0:8], incl_s[:, :], g_tok[0:NS, PT, :], start=True, stop=True)
            e.matmul(ps[0:NS, 1, 8:16], same_s[:, :], g_tok[0:NS, PT, :], start=True, stop=True)
            e.matmul(ps[:, 0, 64:128], ones[0:NS, :], g_own[0:NS, :], start=True, stop=True).then_inc(sem("tensor_stage"), reached("cum_psum"))
            e.wait_ge(sem("vector_stage"), nth["cum_out"])
            e.wait_ge(sem("scalar_stage"), nth["tail_rows"])
            with e.Fori(0, 2) as gp:
                with e.Fori(0, PT) as c:
                    pe_chunk(e, gp, gp * PT + c, "")
                e.wait_ge(sem("mixed_c"), PRIMED + gp * PT + PT)
                for j in range(GH):
                    mm = e.transpose(ps[:, 5, j * P:(j + 1) * P], state[:, j, :], ident[:, :])
                mm.then_inc(sem("final_psum"), 1)
            for gp in range(2):
                pe_chunk(e, gp, gp, "_s")
            e.wait_ge(sem("mixed_parts"), KD)
            pe_y(e, gemms["c_out"], 0)

        CP, CS = C_CONV - 1 + SEQ, C_CONV - 1 + DEC_S
        CW = CP + DEC_B * CS
        flat_scr = scr[:, :, :].rearrange("p a t -> p (a t)")

        def ext(m):
            return flat_scr[:, (m % 2) * CW:(m % 2 + 1) * CW]

        def ext_s(m):
            return ext(m)[:, CP:CW].rearrange("p (b t) -> p b t", t=CS)

        def act_c(e):
            def lead(e):
                e.wait_ge(sem("gpsimd_stage"), nth["c_constants_ready"])
                e.copy(halves(ba_t[:, :]), cols(6)).then_inc(sem("lead_ready"), 1)

            e.preload_act_table(ACT.Silu)
            first = proj_count(gemms["c_qkv"])

            def silu_out(i, j):
                m = i * 4 + j
                e.wait_ge(sem("conv_acc"), i * 4 + (j + 1))
                acc = conv_acc[:, j % 2, :]
                e.activation(qkv[:, bass.ds(m, 1), 0:SEQ].rearrange("p o t -> p (o t)"), acc[:, 0:SEQ], ACT.Silu)
                e.activation(qkv[:, bass.ds(m, 1), SEQ:T].rearrange("p o (b t) -> p (o b) t", t=DEC_S),
                             acc[:, CP:CW].rearrange("p (b t) -> p b t", t=CS)[:, :, 0:DEC_S],
                             ACT.Silu).then_inc(sem("conv_ready"), 1)

            def out(e, i, j):
                if j >= 2:
                    e.wait_ge(sem("conv_acc"), i * 4 + (j - 1))
                else:
                    e.wait_ge(sem("ext_free"), i * 2 + j + 1)
                bank = 2 * j
                e.copy(ext(j)[:, 3:3 + TH], ps[:, bank, 0:TH])
                e.copy(ext(j)[:, 3 + TH:CP], ps[:, bank + 1, 0:TH - NS])
                e.copy(ext_s(j)[:, :, 3:CS], ps[:, bank + 1, TH - NS:TH].rearrange("p (b t) -> p b t", t=DEC_S)
                       ).then_inc(sem("proj_ready"), 1)
                if j >= 1:
                    silu_out(i, j - 1)
                if j == 3:
                    silu_out(i, 3)

            act_proj(e, gemms["c_qkv"], out, lead)

            def z_out(e, i, j):
                e.activation(z_t[:, bass.ds(i * 4 + j, 1), :].rearrange("p o (h t) -> p (o h) t", h=2), cols(2 * j),
                             ACT.Silu).then_inc(sem("proj_ready"), 1)

            act_proj(e, gemms["c_z"], z_out)
            e.wait_ge(sem("tensor_stage"), nth["tail_psum"])
            e.copy(tail_rows[:, 0:1536].rearrange("p (x n) -> p x n", x=3), ps[0:27, 2:5, :])
            e.copy(tail_rows[:, 1536:3072].rearrange("p (x n) -> p x n", x=3), ps[0:27, 5:8, :]).then_inc(sem("scalar_stage"), reached("tail_rows"))
            e.preload_act_table_set("natural_log_exp_and_others")
            e.wait_ge(sem("vector_stage"), nth["c_gate_abs"])
            e.activation(gt[1], gt[1], ACT.Exp)
            e.activation(beta, beta, ACT.Exp, scale=-1.0)
            e.activation(a_log, a_log, ACT.Exp).then_inc(sem("scalar_stage"), reached("c_gate_exp"))
            e.wait_ge(sem("vector_stage"), nth["c_gate_exp1"])
            e.activation(gt[3], gt[2], ACT.Ln).then_inc(sem("scalar_stage"), reached("c_gate_log"))
            e.wait_ge(sem("vector_stage"), nth["c_exponents"])
            e.activation(e_G, e_G, ACT.Exp)
            e.activation(e_kd, e_kd, ACT.Exp)
            e.activation(e_last_s, e_last_s, ACT.Exp)
            e.activation(e_last, e_last, ACT.Exp).then_inc(sem("scalar_stage"), reached("c_decays"))
            e.wait_ge(sem("tail_stored"), 32)
            with e.Fori(0, 2) as gp:
                with e.Fori(0, PT) as c:
                    act_chunk(e, gp * PT + c, "")
                e.wait_ge(sem("final_psum"), PRIMED + gp + 1)
                e.wait_ge(sem("final_stored"), PRIMED + gp * 16)
                e.copy(s_final[:, :, :].rearrange("p h k -> p (h k)"), ps[:, 5, :]).then_inc(sem("final_state"), 1)
            for gp in range(2):
                act_chunk(e, gp, "_s")
            e.wait_ge(sem("mixed_c"), PRIMED + 2 * PT + 2)
            for k in range(KD):
                e.copy(hd_hi[:, k, :], z_t[:, k, :]).then_inc(sem("mixed_hi"), 1)
            e.wait_ge(sem("states_stored"), 16 * 8)
            act_y(e, gemms["c_out"], y_mix)

        def act_chunk(e, it, sfx):
            n = NS if sfx else P
            per = levels_of(sfx) - 1

            def wait(name, k=1, each=1):
                e.wait_ge(sem(name), chunks_before(name, sfx) + it * each + k)

            bank = lambda x, w: ps[0:n, x, 0:GH * w].rearrange("p (h t) -> p h t", h=GH)
            wait("tok_psum")
            e.activation(scr[0:n, 0, 0:GH * P], ps[0:n, 2, :], ACT.Square)
            e.activation(scr[0:n, 2, 0:GH * P], ps[0:n, 1, :], ACT.Square).then_inc(sem("sq_ready"), 1)
            e.copy(tok_v[0:n], bank(0, P)).then_inc(sem("v_ready"), 1)
            wait("decay_psum")
            e.activation(e_mat[0:n, :, 0:n], bank(7, n), ACT.Exp).then_inc(sem("e_ready"), 1)
            wait("feat_psum")
            for b, t in ((3, kq_t[:, 0]), (4, kq_t[:, 1])):
                ins = e.copy(t[:, :, 0:n], ps[:, b, 0:GH * n].rearrange("p (h t) -> p h t", h=GH))
            ins.then_inc(sem("feat_ready"), 1)
            if sfx:
                for j in range(GH):
                    e.wait_ge(sem("states_psum"), it * GH + j + 1)
                    e.copy(s_turned[:, j, 0:4, :].rearrange("p b v -> p (b v)"), ps[:, 4 + 2 * (j % 2), :]).then_inc(sem("turned_a"), 1)
                e.wait_ge(sem("kq_psum"), it + 1)
                e.copy(kq_s[:, :, :, :].rearrange("p x j t -> p (x j t)"), ps[:, 0, 0:2 * GH * NS]).then_inc(sem("kq_ready"), 1)
            wait("x0_psum")
            e.copy(x_m[0:n, :, 0:n], bank(2, n)).then_inc(sem("x0_ready"), 1)
            for l in range(1, levels_of(sfx)):
                for hf in range(2):
                    wait("t1_psum", 2 * (l - 1) + hf + 1, 2 * per)
                    e.copy(t1[0:n, 2 * hf:2 * hf + 2, 0:n], bank(2 + hf, n)[:, 2 * hf:2 * hf + 2]).then_inc(sem("t1_ready"), 1)
            wait("u_psum")
            e.copy(u_vec[0:n], bank(1, P)).then_inc(sem("u_ready"), 1)
            wait("o_psum")
            e.activation(scr[0:n, 0, 0:GH * P], ps[0:n, 2, :], ACT.Square).then_inc(sem("osq_ready"), 1)

        def dve_c_first(e):
            e.wait_ge(sem("tensor_stage"), nth["hist_psum"])
            e.tensor_copy(hist[:, :].rearrange("p (x n) -> p x n", x=2), ps[:, 4:6, 0:288])
            e.tensor_copy(c_w[:, :], ps[:, 2, 0:96]).then_inc(sem("vector_stage"), reached("hist_out"))
            e.wait_ge(sem("vector_stage"), nth["hist_out"])

        def dve_c(e):
            def conv(e, i, j):
                m = i * 4 + j
                es = ext_s(j)
                hm = hist[:, bass.ds(m * 24, 24)].rearrange("p (b t) -> p b t", t=3)
                step = [0]

                def own(ins):
                    step[0] += 1
                    ins.then_inc(sem("conv_step"), 1)
                    e.wait_ge(sem("conv_step"), i * 20 + j * 5 + step[0])

                e.wait_ge(sem("proj_ready"), first + i * 4 + (j + 1))
                own(e.tensor_copy(es[:, :, 0:3], hm))
                e.tensor_copy(tail[:, bass.ds(m, 1), 0:3].rearrange("p o t -> p (o t)"), ext(j)[:, SEQ:CP])
                e.tensor_copy(tail[:, bass.ds(m, 1), 3:27].rearrange("p o (b t) -> p (o b) t", t=3), es[:, :, DEC_S:CS])
                acc = conv_acc[:, j % 2, 0:CW - 3]
                w = lambda x: c_w[:, bass.ds(m + 24 * x, 1)]
                own(e.tensor_scalar(acc, ext(j)[:, 0:CW - 3], w(0), None, ALU.mult))
                for x in range(1, 3):
                    own(e.scalar_tensor_tensor(acc, ext(j)[:, x:x + CW - 3], w(x), acc, ALU.mult, ALU.add))
                own(e.scalar_tensor_tensor(acc, ext(j)[:, 3:CW], w(3), acc, ALU.mult, ALU.add))
                if j >= 2:
                    e.tensor_copy(small[:, 34 + j:35 + j], acc[:, 0:1]).then_inc(sem("ext_free"), 1)
                e.tensor_copy(small[:, 40 + j:41 + j], acc[:, 1:2]).then_inc(sem("conv_acc"), 1)

            first = proj_count(gemms["c_qkv"])
            e.wait_ge(sem("hd_lo_ready"), KD * (subs.index(("c", 1, 0)) + 1))
            for x in range(2):
                e.memset(ext(x)[:, 0:3], 0.0).then_inc(sem("ext_free"), 1)
            dve_proj(e, gemms["c_qkv"], conv)
            dve_proj(e, gemms["c_z"])

            e.wait_ge(sem("tensor_stage"), nth["ba_psum"])
            e.wait_ge(sem("c_small_in"), 48)
            e.wait_ge(sem("lead_ready"), lead_c)
            src = ps[:, 0, :].rearrange("p (c n) -> p c n", c=PT)
            e.tensor_copy(beta[:, 0:PT * 8].rearrange("p (c h) -> p c h", h=8), src[:, :, P - 16:P - 8])
            e.tensor_copy(beta[0:NS, PT * 8:], ps[0:NS, 1, P - 16:P - 8])
            e.tensor_copy(gt[0][:, 0:PT * 8].rearrange("p (c h) -> p c h", h=8), src[:, :, P - 8:P])
            chain(e, e.tensor_copy(gt[0][0:NS, PT * 8:], ps[0:NS, 1, P - 8:P]))
            by_tile = lambda t: t.rearrange("p (c h) -> p c h", h=8)
            rows8 = lambda t: t.unsqueeze(1).to_broadcast([P, PT + 1, 8])
            chain(e, e.tensor_tensor(by_tile(gt[0]), by_tile(gt[0]), rows8(dt_bias), ALU.add))
            chain(e, e.tensor_scalar(gt[1], gt[0], -1.0, None, ALU.mult))
            e.tensor_tensor(gt[1], gt[1], gt[0], ALU.min).then_inc(sem("vector_stage"), reached("c_gate_abs"))
            e.wait_ge(sem("scalar_stage"), nth["c_gate_exp"])
            e.tensor_scalar(gt[2], gt[1], 1.0, None, ALU.add).then_inc(sem("vector_stage"), reached("c_gate_exp1"))
            chain(e, e.tensor_scalar(beta, beta, 1.0, None, ALU.add))
            chain(e, e.reciprocal(beta, beta))
            e.wait_ge(sem("scalar_stage"), nth["c_gate_log"])
            chain(e, e.scalar_tensor_tensor(gt[3], gt[3], TINY, gt[1], ALU.add, ALU.mult))
            chain(e, e.tensor_scalar(gt[2], gt[2], -1.0, TINY, ALU.add, ALU.add))
            chain(e, e.reciprocal(gt[1], gt[2]))
            chain(e, e.tensor_tensor(gt[3], gt[3], gt[1], ALU.mult))
            chain(e, e.scalar_tensor_tensor(gt[3], gt[0], 0.0, gt[3], ALU.max, ALU.add))
            chain(e, e.scalar_tensor_tensor(g_tok[:, :, :], by_tile(gt[3]), -1.0, rows8(a_log), ALU.mult, ALU.mult))
            e.tensor_tensor(g_own[0:NS, :].rearrange("p (b h) -> p b h", h=8),
                            g_tok[0:NS, PT, :].unsqueeze(1).to_broadcast([NS, DEC_B, 8]),
                            own_s[:, :].unsqueeze(2).to_broadcast([NS, DEC_B, 8]), ALU.mult).then_inc(sem("vector_stage"), reached("g_ready"))
            e.wait_ge(sem("tensor_stage"), nth["cum_psum"])
            e.tensor_copy(e_G[:, 0:32], ps[:, 0, 0:32])
            e.tensor_copy(e_last, ps[:, 0, 32:64])
            e.tensor_copy(e_last_s, ps[:, 0, 64:128])
            e.tensor_copy(e_G[0:NS, 32:40], ps[0:NS, 1, 0:8])
            chain(e, e.tensor_copy(e_kd[0:NS, 32:40], ps[0:NS, 1, 8:16]))
            e.tensor_tensor(e_kd[:, 0:32], e_last, e_G[:, 0:32], ALU.subtract)
            e.tensor_tensor(e_kd[0:NS, 32:40], e_kd[0:NS, 32:40], e_G[0:NS, 32:40], ALU.subtract).then_inc(sem("vector_stage"), reached("c_exponents"))
            e.wait_ge(sem("scalar_stage"), nth["c_decays"])
            chain(e, e.tensor_scalar(n_G, e_G, -1.0, None, ALU.mult))
            e.wait_ge(sem("tail_stored"), 32)
            e.tensor_copy(small[:, 50:51], n_G[:, 0:1]).then_inc(sem("vector_stage"), reached("cum_out"))
            with e.Fori(0, 2) as gp:
                e.wait_ge(sem("final_psum"), PRIMED + gp)
                e.memset(state[:, :, :], 0.0).then_inc(sem("state_ready"), 1)
                with e.Fori(0, PT) as c:
                    dve_chunk(e, gp, c, gp * PT + c, "")
            for gp in range(2):
                dve_chunk(e, gp, PT, gp, "_s")
            for k in range(KD):
                e.wait_ge(sem("mixed_hi"), k + 1)
                e.tensor_tensor(hd_lo[:, k, :], z_t[:, k, :], hd_hi[:, k, :].bitcast(F32),
                                ALU.subtract).then_inc(sem("mixed_parts"), 1)
            dve_y(e, gemms["c_out"])

        def dve_chunk(e, gp, c, it, sfx):
            n = NS if sfx else P
            per = levels_of(sfx) - 1
            steps = PER_CHUNK["chunk_step"]
            step = [0]

            def own(ins):
                step[0] += 1
                ins.then_inc(sem("chunk_step"), 1)
                e.wait_ge(sem("chunk_step"), chunks_before("chunk_step", sfx) + it * steps + step[0])

            def wait(name, k=1, each=1):
                e.wait_ge(sem(name), chunks_before(name, sfx) + it * each + k)

            heads = bass.ds(c * 8 + gp * GH, GH)
            each_head = lambda t, w: t.unsqueeze(2).to_broadcast([n, GH, w])
            mask_of = lambda m: m.unsqueeze(1).to_broadcast([n, GH, n])
            bank = lambda x, w: ps[0:n, x, 0:GH * w].rearrange("p (h t) -> p h t", h=GH)
            tri = incl_s[:, :] if sfx else incl[:, :]

            g_col = g_tok[:, :, :].rearrange("p c h -> p (c h)")[0:n, heads]
            e.tensor_tensor(scr[0:n, 1, 0:GH * n].rearrange("p (h t) -> p h t", h=GH), mask_of(tri), each_head(g_col, n),
                            ALU.mult).then_inc(sem("g_masked"), 1)
            wait("sq_ready")
            sq = lambda x: scr[0:n, x, 0:GH * P].rearrange("p (h d) -> p h d", h=GH)
            e.tensor_reduce(nrm[0:n, 0:GH], sq(0), AX.X, ALU.add)
            own(e.tensor_reduce(nrm[0:n, GH:2 * GH], sq(2), AX.X, ALU.add))
            own(e.tensor_scalar(nrm[0:n], nrm[0:n], EPS, None, ALU.add))

            def rsq(out, tmp, x):
                own(e.tensor_scalar(tmp.bitcast(I32), x.bitcast(I32), 1, None, ALU.arith_shift_right))
                own(e.tensor_scalar(out.bitcast(I32), tmp.bitcast(I32), -1, MAGIC, ALU.mult, ALU.add))
                for _ in range(3):
                    own(e.tensor_tensor(tmp, out, out, ALU.mult))
                    own(e.scalar_tensor_tensor(tmp, tmp, -0.5, x, ALU.mult, ALU.mult))
                    own(e.scalar_tensor_tensor(out, tmp, 1.5, out, ALU.add, ALU.mult))

            rs, tmp = nrm_r[0:n], nrm_t[0:n]
            rsq(rs, tmp, nrm[0:n])
            rq, rk = rs[:, 0:GH], rs[:, GH:2 * GH]
            own(e.tensor_scalar(rq, rq, P ** -0.5, None, ALU.mult))
            f = [fac[0:n, x * GH:(x + 1) * GH] for x in range(3)]
            e.tensor_tensor(f[0], rq, e_G[0:n, heads], ALU.mult)
            e.tensor_tensor(f[1], rk, beta[0:n, heads], ALU.mult)
            own(e.tensor_tensor(f[2], rk, e_kd[0:n, heads], ALU.mult))
            e.tensor_tensor(tok_k[0:n], bank(1, P), each_head(rk, P), ALU.mult)
            e.tensor_tensor(tok_kb[0:n], bank(1, P), each_head(f[1], P), ALU.mult)
            e.tensor_tensor(tok_kd[0:n], bank(1, P), each_head(f[2], P), ALU.mult)
            e.tensor_tensor(tok_qd[0:n], bank(2, P), each_head(f[0], P), ALU.mult)
            e.tensor_tensor(tok_q[0:n], bank(2, P), each_head(rq, P), ALU.mult).then_inc(sem("tok_scaled"), 1)
            wait("feat_psum")
            for b, t in ((5, q_t), (6, kb_t)):
                ins = e.tensor_copy(t[:, :, 0:n], ps[:, b, 0:GH * n].rearrange("p (h t) -> p h t", h=GH))
            ins.then_inc(sem("feat_b_ready"), 1)
            wait("e_ready")
            em = e_mat[0:n, :, 0:n]
            own(e.tensor_tensor(em, em, mask_of(tri), ALU.mult))
            wait("kk_psum")
            own(e.tensor_tensor(u_mat[0:n, :, 0:n], bank(0, n), em, ALU.mult))
            e.tensor_tensor(p_t[0:n, :, 0:n], bank(1, n), em, ALU.mult).then_inc(sem("kk_out"), 1)
            xt = x_t[0:n, :, 0:n]
            own(e.tensor_tensor(xt, u_mat[0:n, :, 0:n], mask_of(halves_m[0:n, 0, 0:n]), ALU.mult))
            e.tensor_tensor(xt, mask_of(ident[0:n, 0:n]), xt, ALU.subtract).then_inc(sem("xt1_ready"), 1)
            if sfx:
                for j in range(GH):
                    e.wait_ge(sem("states_psum"), it * GH + j + 1)
                    e.tensor_copy(s_turned[:, j, 4:8, :].rearrange("p b v -> p (b v)"), ps[:, 5 + 2 * (j % 2), :]
                                  ).then_inc(sem("turned_b"), 1)
            wait("v_ready")
            wait("kr_psum")
            kr = 3 if sfx else 0
            for j in range(GH):
                ng = n_G[0:n, bass.ds(c * 8 + gp * GH + j, 1)]
                ins = e.scalar_tensor_tensor(b_mat[0:n, j, :], bank(kr, P)[:, j], ng, tok_v[0:n, j, :], ALU.mult, ALU.add)
            ins.then_inc(sem("b_ready"), 1)
            wait("x0_ready")
            for l in range(1, levels_of(sfx)):
                for hf in range(2):
                    hs = slice(2 * hf, 2 * hf + 2)
                    wait("x_step_psum", 2 * (l - 1) + hf + 1, 2 * per)
                    if l < per:
                        e.tensor_tensor(x_m[0:n, hs, 0:n], x_m[0:n, hs, 0:n], bank(4 + hf, n)[:, hs], ALU.subtract)
                    e.tensor_tensor(x_t[0:n, hs, 0:n], x_t[0:n, hs, 0:n], bank(6 + hf, n)[:, hs],
                                    ALU.subtract).then_inc(sem("x_step"), 1)
            wait("x_step", 2 * per, 2 * per)
            e.tensor_tensor(xt, xt, each_head(beta[0:n, heads], n), ALU.mult).then_inc(sem("xb_ready"), 1)
            if sfx:
                for j in range(GH):
                    if j >= 2:
                        e.wait_ge(sem("ds_psum"), it * GH + j - 1)
                    e.tensor_tensor(kd_m[0:n, j % 2, :, :], tok_kd[0:n, j, :].unsqueeze(1).to_broadcast([n, DEC_B, P]),
                                    own_s[:, :].unsqueeze(2).to_broadcast([n, DEC_B, P]), ALU.mult).then_inc(sem("kd_masked"), 1)
                    if j >= 1:
                        new_states(e, it, j - 1, gp)
                new_states(e, it, GH - 1, gp)
            wait("osq_ready")
            own(e.tensor_reduce(nrm[0:n, 0:GH], sq(0), AX.X, ALU.add))
            own(e.tensor_scalar(nrm[0:n, 0:GH], nrm[0:n, 0:GH], 1.0 / P, EPS, ALU.mult, ALU.add))
            rsq(rs[:, 0:GH], tmp[:, 0:GH], nrm[0:n, 0:GH])
            e.tensor_tensor(t1[0:n], bank(2, P), each_head(rs[:, 0:GH], P), ALU.mult).then_inc(sem("o_normed"), 1)
            if not sfx:
                wait("dr_psum")
                for j in range(GH):
                    gl = e_last[:, bass.ds(c * 8 + gp * GH + j, 1)]
                    ins = e.scalar_tensor_tensor(state[:, j, :], state[:, j, :], gl, ps[:, 3, j * P:(j + 1) * P],
                                                 ALU.mult, ALU.add)
                ins.then_inc(sem("state_ready"), 1)
            wait("ot_psum")
            where = z_t[:, bass.ds(gp * GH, GH), bass.ds(c * P, n)]
            own(e.scalar_tensor_tensor(where, ps[:, 4, 0:GH * n].rearrange("p (h t) -> p h t", h=GH), norm_w, where,
                                       ALU.mult, ALU.mult))
            assert step[0] == steps, step
            e.memset(small[:, 61:62], 0.0).then_inc(sem("mixed_c"), 1)

        def new_states(e, it, j, gp):
            e.wait_ge(sem("ds_psum"), it * GH + j + 1)
            for b in range(DEC_B):
                gl = e_last_s[:, b * 8 + gp * GH + j:b * 8 + gp * GH + j + 1]
                ins = e.scalar_tensor_tensor(s_all[it][:, j, b, :], s_all[it][:, j, b, :], gl,
                                             ps[:, 6 + b // 4, (b % 4) * P:(b % 4 + 1) * P], ALU.mult, ALU.add)
            ins.then_inc(sem("state_step"), 1)
            if j == GH - 1:
                e.wait_ge(sem("state_step"), it * GH + GH)
                e.memset(small[:, 62:63], 0.0).then_inc(sem("states_out"), 1)

        block = stack.enter_context(nc.Block())

        pre_gain = {("ffn", 0): 0, ("ffn", 1): 4, ("ab", 0): 2, ("c", 0): 2}

        @block.sync
        def _(e):
            e.dma_start(rows_p[:, :, :], io["x_prompt"].rearrange("b (c p) d -> p (b c) d", p=P)).then_inc(sem("rows_in"), 16)
            e.dma_start(rows_s[:, :], io["x_sample"].rearrange("b t d -> (b t) d")).then_inc(sem("sample_rows_in"), 16)
            e.dma_start(gain_rows[:, :], io["norm_g"].rearrange("l n (k p) -> (l n k) p", p=P)).then_inc(sem("gains_in"), 16)
            for kind, l, w in subs:
                if kind == "ffn":
                    sp_gemm(e, gemms[f"gate_up{l}{w}"])
                    sp_gemm(e, gemms[f"down{l}{w}"])
                if kind == "ab":
                    sp_ab(e)
                if kind == "c":
                    sp_c(e)
            e.wait_ge(sem("rows_out"), PT * 2 + 1)
            e.dma_start(io["y_prompt"].rearrange("b (c p) d -> p (b c) d", p=P), rows_p[:, :, :]).then_inc(sem("stored"), 16)
            e.dma_start(io["y_sample"].rearrange("b t d -> (b t) d"), rows_s[:, :]).then_inc(sem("stored"), 16)
            e.wait_ge(sem("stored"), 16 * (2 + 6 * any(x[0] == "ab" for x in subs)))
            if ("ab", 0, 0) in subs:
                e.wait_ge(sem("kv_stored"), PRIMED + 2 * 16 * NP)

        @block.gpsimd
        def _(e):
            for n, name in enumerate(PRIMED_SEMS):
                e.memset(primer[:, n:n + 1], 0.0).then_inc(sem(name), PRIMED)
            e.memset(ident[:, :], 0.0).then_inc(sem("gpsimd_stage"), reached("ident_zero"))
            e.memset(ones[:, :], 1.0).then_inc(sem("gpsimd_stage"), reached("ones_ready"))
            e.wait_ge(sem("gpsimd_stage"), nth["ident_zero"])
            e.affine_select(out=ident[:, :], in_=ident[:, :], compare_op=ALU.not_equal, fill=1.0, base=0,
                            pattern=[[-1, P]], channel_multiplier=1).then_inc(sem("gpsimd_stage"), reached("ident_ready"))
            if any(x[0] == "ab" for x in subs):
                pool_ab(e)
            if any(x[0] == "c" for x in subs):
                pool_c(e)

        @block.tensor
        def _(e):
            e.wait_ge(sem("gpsimd_stage"), nth["ident_ready"])
            e.wait_ge(sem("gpsimd_stage"), nth["ones_ready"])
            e.wait_ge(sem("rows_in"), 16)
            e.wait_ge(sem("sample_rows_in"), 16)
            e.wait_ge(sem("gains_in"), 16)
            n = DEPTH * 6 * KD
            e.transpose(ps[:, 7, 0:n], gain_rows[:, :], ident[0:n, 0:n]).then_inc(sem("tensor_stage"), reached("gains_psum"))
            for k in range(KD):
                if k >= 3:
                    e.wait_ge(sem("x_ready"), k - 2)
                for c in range(PT):
                    e.transpose(ps[:, 2 * (k % 3), c * P:(c + 1) * P], rows_p[:, c, k * P:(k + 1) * P], ident[:, :])
                e.transpose(ps[:, 2 * (k % 3) + 1, 0:NS], rows_s[:, k * P:(k + 1) * P],
                            ident[0:NS, 0:NS]).then_inc(sem("x_psum"), 1)
            e.wait_ge(sem("vector_stage"), nth["gains_ready"])
            pe_squares_x(e, 0)
            for s, (kind, l, w) in enumerate(subs):
                hd_ready_by_chunk[0] = KD * s
                if kind == "ffn":
                    pe_gate_up(e, gemms[f"gate_up{l}{w}"])
                    pe_y(e, gemms[f"down{l}{w}"], 0)
                if kind == "ab":
                    pe_ab(e)
                if kind == "c":
                    pe_c(e)
                pe_squares_x(e, s + 1)
            for c in range(PT + 1):
                for q in range(2):
                    u = 2 * c + q
                    if u >= 4:
                        e.wait_ge(sem("rows_out"), u - 3)
                    if c == PT and q == 1:
                        break
                    if c < PT:
                        for k in range(4):
                            mm = e.transpose(ps[:, u % 4, k * P:(k + 1) * P], xT[:, 4 * q + k, c * P:(c + 1) * P], ident[:, :])
                    else:
                        for k in range(KD):
                            mm = e.transpose(ps[0:NS, 4 + k // 4, (k % 4) * P:(k % 4 + 1) * P], xT[:, k, SEQ:T], ident[:, :])
                    mm.then_inc(sem("rows_psum"), 1)

        @block.scalar
        def _(e):
            act_split(e, 0, 0, KD)
            act_split(e, 1, 0, KD)
            act_squares_x(e, 0)
            for s, (kind, l, w) in enumerate(subs):
                act_norm(e, 2 * s)
                act_pre(e, s)
                if kind == "ffn":
                    act_gate_up(e, gemms[f"gate_up{l}{w}"])
                    act_y(e, gemms[f"down{l}{w}"], y_ffn)
                if kind == "ab":
                    act_ab(e)
                if kind == "c":
                    act_c(e)
                act_norm(e, 2 * s + 1)
                act_squares_x(e, s + 1)

        @block.vector
        def _(e):
            e.wait_ge(sem("tensor_stage"), nth["gains_psum"])
            chain(e, e.tensor_copy(gains[:, :], ps[:, 7, 0:DEPTH * 6 * KD]))
            for l in range(DEPTH):
                for n in (1, 5):
                    at = (l * 6 + n) * KD
                    ins = e.tensor_scalar(gains[:, at:at + KD], gains[:, at:at + KD], 0.5, None, ALU.mult)
                    chain(e, ins)
            e.tensor_copy(small[:, 32:33], gains[:, 0:1]).then_inc(sem("vector_stage"), reached("gains_ready"))
            for k in range(KD):
                e.wait_ge(sem("x_psum"), k + 1)
                e.tensor_copy(xT[:, k, 0:SEQ], ps[:, 2 * (k % 3), :])
                e.tensor_copy(xT[:, k, SEQ:T], ps[:, 2 * (k % 3) + 1, 0:NS]).then_inc(sem("x_ready"), 1)
            dve_split(e, 0, 0, KD)
            dve_split(e, 1, 0, KD)
            for s, (kind, l, w) in enumerate(subs):
                dve_norm(e, 2 * s)
                dve_pre(e, s, l, pre_gain[kind, w])
                if kind == "c":
                    dve_c_first(e)
                if kind == "ffn":
                    dve_gate_up(e, gemms[f"gate_up{l}{w}"])
                    dve_y(e, gemms[f"down{l}{w}"])
                if kind == "ab":
                    dve_ab(e)
                if kind == "c":
                    dve_c(e)
                dve_norm(e, 2 * s + 1)
                dve_post(e, s, l, pre_gain[kind, w] + 1, y_ffn if kind == "ffn" else y_mix)
            for c in range(PT):
                for q in range(2):
                    u = 2 * c + q
                    e.wait_ge(sem("rows_psum"), u + 1)
                    e.tensor_copy(rows_p[:, c, 4 * q * P:4 * (q + 1) * P], ps[:, u % 4, :]).then_inc(sem("rows_out"), 1)
            e.wait_ge(sem("rows_psum"), 2 * PT + 1)
            e.tensor_copy(rows_s[:, :].rearrange("p (a n) -> p a n", a=2), ps[0:NS, 4:6, :]).then_inc(sem("rows_out"), 1)


_INS = ["x_prompt", "x_sample", "cache_a_k", "cache_a_v", "cache_a_logf", "page_table", "state_b_conv",
        "state_c_conv", "state_c_S", "norm_g", "ffn_w_gate", "ffn_w_up", "ffn_w_down", "ab_w_in", "ab_b_f",
        "ab_conv_w", "ab_w_out", "c_w_in", "c_conv_w", "c_a_log", "c_dt_bias", "c_norm_w", "c_w_out"]
_OUTS = {
    "y_prompt": (1, SEQ, D_MODEL),
    "y_sample": (DEC_B, DEC_S, D_MODEL),
    "a_k_prompt": (1, 1, SEQ, A_HEADS, A_DIM),
    "a_v_prompt": (1, 1, SEQ, A_HEADS, A_DIM),
    "a_logf_prompt": (1, 1, SEQ, A_HEADS),
    "a_k_sample": (1, DEC_B, DEC_S, A_HEADS, A_DIM),
    "a_v_sample": (1, DEC_B, DEC_S, A_HEADS, A_DIM),
    "a_logf_sample": (1, DEC_B, DEC_S, A_HEADS),
    "b_conv_prompt": (1, 1, B_CONV - 1, B_WIDTH),
    "b_conv_sample": (1, DEC_B, B_CONV - 1, B_WIDTH),
    "c_conv_prompt": (1, 1, C_CONV - 1, 3 * D_MODEL),
    "c_conv_sample": (1, DEC_B, C_CONV - 1, 3 * D_MODEL),
    "c_S_prompt": (1, 1, C_HEADS, P, P),
    "c_S_sample": (1, DEC_B, C_HEADS, P, P),
}


def kernel(**inputs):
    import concourse.bacc as _bacc
    from concourse.bass_utils import run_bass_kernel_spmd as _run

    nc = _bacc.Bacc("TRN2", target_bir_lowering=False, num_devices=1)
    arrays, io = {}, {}
    for name in _INS:
        a = np.ascontiguousarray(inputs[name])
        arrays[f"in_{name}_dram"] = a
        io[name] = nc.dram_tensor(f"in_{name}_dram", a.shape, mybir.dt.from_np(a.dtype), kind="ExternalInput").ap()
    for i, (name, shape) in enumerate(_OUTS.items()):
        io[name] = nc.dram_tensor(f"out_{i}_dram", shape, F32, kind="ExternalOutput").ap()
    build(nc, io)
    r = _run(nc, [arrays], core_ids=[0])
    return tuple(np.asarray(r.results[0][f"out_{i}_dram"]) for i in range(len(_OUTS)))
```
